# Optimizing a Trainium2 kernel written in Bass

```python
import jax, jax.numpy as jnp
from jax import lax
import numpy as np

D_MODEL = 1024
BATCH = 1
SEQ = 1024
DEPTH = 2
DEC_BATCH = 1
DEC_SEQ = 256
PAST_LEN = 128

GRID_W = 64
N_MIXERS = 2
N_HEADS = 16
HEAD_DIM = D_MODEL // N_HEADS
WIN_H = 8
WIN_W = 16
Q_COL_BLOCK = 16
K_COL_SPAN = Q_COL_BLOCK + WIN_W
N_COL_BLOCKS = GRID_W // Q_COL_BLOCK
RPB_H = 2 * WIN_H - 1
RPB_W = 2 * WIN_W - 1
D_FF = 2816
CONV_W = 3
LORA_DECAY = 64
LORA_ICLR = 64
LORA_VALUE = 32
LORA_GATE = 160
N_A_LAYERS = (DEPTH + 1) // 2
N_B_LAYERS = DEPTH // 2
RMS_EPS = 1e-6
GN_EPS = 64e-5
NEG_INF = -1e30

kernel_name = "hybrid_natten_rwkv7_convffn_encoder"

def _rms(x, g):
    xf = x.astype(jnp.float32)
    y = xf * lax.rsqrt(jnp.mean(xf * xf, axis=-1, keepdims=True) + RMS_EPS)
    return (y * g.astype(jnp.float32)).astype(x.dtype)

def _na_indices(rows):
    kh = min(WIN_H, rows)
    r = np.arange(rows)
    rs = np.clip(r - kh // 2, 0, rows - kh)
    row_idx = rs[:, None] + np.arange(kh)[None, :]
    jb = np.arange(N_COL_BLOCKS)
    cb = np.clip(jb * Q_COL_BLOCK - WIN_W // 2, 0, GRID_W - K_COL_SPAN)
    col_idx = cb[:, None] + np.arange(K_COL_SPAN)[None, :]
    c = np.arange(GRID_W).reshape(N_COL_BLOCKS, Q_COL_BLOCK)
    cs = np.clip(c - WIN_W // 2, 0, GRID_W - WIN_W)
    kc = col_idx[:, None, :]
    col_ok = (kc >= cs[..., None]) & (kc < cs[..., None] + WIN_W)
    d_row = row_idx - r[:, None] + WIN_H - 1
    d_col = np.clip(kc - c[..., None] + WIN_W - 1, 0, RPB_W - 1)
    return row_idx, col_idx, col_ok, d_row, d_col

def neighbourhood_attention(h, w_qkv, w_o, q_gain, k_gain, rpb):
    b, s, d = h.shape
    rows = s // GRID_W
    row_idx, col_idx, col_ok, d_row, d_col = _na_indices(rows)
    qkv = (h @ w_qkv).reshape(b, rows, GRID_W, 3, N_HEADS, HEAD_DIM)
    q = _rms(qkv[:, :, :, 0], q_gain) * (HEAD_DIM ** -0.5)
    k = _rms(qkv[:, :, :, 1], k_gain)
    v = qkv[:, :, :, 2]
    q = q.reshape(b, rows, N_COL_BLOCKS, Q_COL_BLOCK, N_HEADS, HEAD_DIM)
    ri = row_idx[:, :, None, None]
    ci = col_idx[None, None, :, :]
    kb = k[:, ri, ci]
    vb = v[:, ri, ci]
    sc = jnp.einsum('brjqhd,brijchd->brjhqic', q, kb, preferred_element_type=jnp.float32)
    bias = rpb.astype(jnp.float32)[:, d_row[:, None, None, :, None], d_col[None, :, :, None, :]]
    bias = jnp.transpose(bias, (1, 2, 0, 3, 4, 5))
    mask = col_ok[:, None, :, None, :]
    sc = jnp.where(mask, sc + bias, NEG_INF)
    p = jax.nn.softmax(sc, axis=(-2, -1)).astype(v.dtype)
    o = jnp.einsum('brjhqic,brijchd->brjqhd', p, vb)
    return o.reshape(b, s, d) @ w_o

def _centred_shift(x):
    prev = jnp.pad(x[:, :-1], ((0, 0), (1, 0), (0, 0)))
    nxt = jnp.pad(x[:, 1:], ((0, 0), (0, 1), (0, 0)))
    return 0.5 * (prev + nxt) - x

def _heads(z):
    return z.reshape(z.shape[:-1] + (N_HEADS, HEAD_DIM))

def _flip_bwd(z):
    return jnp.stack([z[0], jnp.flip(z[1], axis=1)])

def _wkv7_step(S, inp):
    r_t, w_t, k_t, v_t, aa_t, bb_t = inp
    sa = jnp.einsum('zbhij,zbhj->zbhi', S, aa_t)
    S = S * w_t[..., None, :] + sa[..., :, None] * bb_t[..., None, :] + v_t[..., :, None] * k_t[..., None, :]
    y = jnp.einsum('zbhij,zbhj->zbhi', S, r_t)
    return S, y

def rwkv7_mixer(h, v_first, vres, mu, w_r, w_k, w_v, w_o, w0, w1, w2, a0, a1, a2, g1, g2, k_k, k_a, r_k, ln_w, ln_b):
    b, t, d = h.shape
    f32 = jnp.float32
    xx = _centred_shift(h)
    xr, xw, xk, xv, xa, xg = (h + xx * mu[i] for i in range(6))
    r = xr @ w_r
    k = xk @ w_k
    v = xv @ w_v
    if vres is None:
        v_first = v
    else:
        v0, v1, v2 = vres
        v = v + (v_first - v) * jax.nn.sigmoid(v0 + (xv @ v1) @ v2)
    g = jax.nn.sigmoid(xg @ g1) @ g2
    lw = jnp.einsum('zbtl,zld->zbtd', jnp.tanh(jnp.einsum('btd,zdl->zbtl', xw, w1)), w2)
    w_raw = -jax.nn.softplus(-(w0[:, None, None].astype(f32) + lw.astype(f32))) - 0.5
    decay = jnp.exp(-jnp.exp(w_raw))
    la = jnp.einsum('zbtl,zld->zbtd', jnp.einsum('btd,zdl->zbtl', xa, a1), a2)
    a = jax.nn.sigmoid(a0[:, None, None].astype(f32) + la.astype(f32))
    kk = _heads((k * k_k).astype(f32))
    kk = kk / jnp.maximum(jnp.sqrt(jnp.sum(kk * kk, axis=-1, keepdims=True)), 1e-12)
    k_dir = k.astype(f32)[None] * (1.0 + (a - 1.0) * k_a.astype(f32))
    a_h, k_h, w_h = _heads(a), _heads(k_dir), _heads(decay)
    r_h, v_h = _heads(r.astype(f32)), _heads(v.astype(f32))
    dshape = (2,) + r_h.shape
    r2 = jnp.broadcast_to(r_h, dshape)
    v2 = jnp.broadcast_to(v_h, dshape)
    aa = jnp.broadcast_to(-kk, dshape)
    bb = kk[None] * a_h
    seq = tuple(jnp.moveaxis(_flip_bwd(z), 2, 0) for z in (r2, w_h, k_h, v2, aa, bb))
    S0 = jnp.zeros((2, b, N_HEADS, HEAD_DIM, HEAD_DIM), f32)
    _, ys = lax.scan(_wkv7_step, S0, seq)
    y = jnp.sum(_flip_bwd(jnp.moveaxis(ys, 0, 2)), axis=0)
    mean = jnp.mean(y, axis=-1, keepdims=True)
    var = jnp.mean(jnp.square(y - mean), axis=-1, keepdims=True)
    yn = ((y - mean) * lax.rsqrt(var + GN_EPS)).reshape(b, t, d) * ln_w.astype(f32) + ln_b.astype(f32)
    bonus = jnp.sum(jnp.sum(r_h[None] * k_h * r_k.astype(f32), axis=-1, keepdims=True), axis=0) * v_h
    out = ((yn + bonus.reshape(b, t, d)) * g.astype(f32)).astype(h.dtype) @ w_o
    return out, v_first

def conv_ffn(h, w_gate, w_up, conv_w, conv_b, w_down):
    gt = h @ w_gate
    gp = jnp.pad(gt, ((0, 0), (1, 1), (0, 0)))
    gc = gp[:, :-2] * conv_w[0] + gp[:, 1:-1] * conv_w[1] + gp[:, 2:] * conv_w[2] + conv_b
    return (jax.nn.silu(gc) * (h @ w_up)) @ w_down

def _trunk(x, norm_mix, norm_ffn, na_w_qkv, na_w_o, na_q_gain, na_k_gain, na_rpb,
           rw_mu, rw_w_r, rw_w_k, rw_w_v, rw_w_o, rw_w0, rw_w1, rw_w2, rw_a0, rw_a1, rw_a2,
           rw_v0, rw_v1, rw_v2, rw_g1, rw_g2, rw_k_k, rw_k_a, rw_r_k, rw_ln_w, rw_ln_b,
           ffn_w_gate, ffn_w_up, ffn_conv_w, ffn_conv_b, ffn_w_down):
    v_first = None
    for i in range(DEPTH):
        hn = _rms(x, norm_mix[i])
        li = i // N_MIXERS
        if i % N_MIXERS == 0:
            x = x + neighbourhood_attention(hn, na_w_qkv[li], na_w_o[li], na_q_gain[li], na_k_gain[li], na_rpb[li])
        else:
            vres = None if li == 0 else (rw_v0[li - 1], rw_v1[li - 1], rw_v2[li - 1])
            out, v_first = rwkv7_mixer(hn, v_first, vres, rw_mu[li], rw_w_r[li], rw_w_k[li], rw_w_v[li], rw_w_o[li],
                                       rw_w0[li], rw_w1[li], rw_w2[li], rw_a0[li], rw_a1[li], rw_a2[li],
                                       rw_g1[li], rw_g2[li], rw_k_k[li], rw_k_a[li], rw_r_k[li], rw_ln_w[li], rw_ln_b[li])
            x = x + out
        x = x + conv_ffn(_rms(x, norm_ffn[i]), ffn_w_gate[i], ffn_w_up[i], ffn_conv_w[i], ffn_conv_b[i], ffn_w_down[i])
    return x

def setup_inputs(seed: int = 0) -> dict:
    key = jax.random.key(seed)
    ks = iter(jax.random.split(key, 48))

    def nrm(shape, scale):
        return jax.random.normal(next(ks), shape, jnp.float32) * scale

    def unif(shape, lo, hi):
        return jax.random.uniform(next(ks), shape, jnp.float32, lo, hi)

    D, F, H, N = D_MODEL, D_FF, N_HEADS, HEAD_DIM
    nA, nB = N_A_LAYERS, N_B_LAYERS
    return {
        "x_prompt": nrm((BATCH, SEQ, D), 1.0),
        "x_sample": nrm((DEC_BATCH, DEC_SEQ, D), 1.0),
        "norm_mix": 1.0 + nrm((DEPTH, D), 0.05),
        "norm_ffn": 1.0 + nrm((DEPTH, D), 0.05),
        "na_w_qkv": nrm((nA, D, 3 * D), D ** -0.5),
        "na_w_o": nrm((nA, D, D), D ** -0.5),
        "na_q_gain": 1.0 + nrm((nA, N), 0.05),
        "na_k_gain": 1.0 + nrm((nA, N), 0.05),
        "na_rpb": nrm((nA, H, RPB_H, RPB_W), 0.5),
        "rw_mu": unif((nB, 6, D), 0.0, 1.0),
        "rw_w_r": nrm((nB, D, D), D ** -0.5),
        "rw_w_k": nrm((nB, D, D), D ** -0.5),
        "rw_w_v": nrm((nB, D, D), D ** -0.5),
        "rw_w_o": nrm((nB, D, D), D ** -0.5),
        "rw_w0": unif((nB, 2, D), -6.0, -1.0),
        "rw_w1": nrm((nB, 2, D, LORA_DECAY), D ** -0.5),
        "rw_w2": nrm((nB, 2, LORA_DECAY, D), 0.5 * LORA_DECAY ** -0.5),
        "rw_a0": nrm((nB, 2, D), 0.1),
        "rw_a1": nrm((nB, 2, D, LORA_ICLR), D ** -0.5),
        "rw_a2": nrm((nB, 2, LORA_ICLR, D), 0.5 * LORA_ICLR ** -0.5),
        "rw_v0": 1.0 + nrm((nB - 1, D), 0.1),
        "rw_v1": nrm((nB - 1, D, LORA_VALUE), D ** -0.5),
        "rw_v2": nrm((nB - 1, LORA_VALUE, D), 0.5 * LORA_VALUE ** -0.5),
        "rw_g1": nrm((nB, D, LORA_GATE), D ** -0.5),
        "rw_g2": nrm((nB, LORA_GATE, D), LORA_GATE ** -0.5),
        "rw_k_k": 0.85 + nrm((nB, D), 0.05),
        "rw_k_a": 1.0 + nrm((nB, D), 0.05),
        "rw_r_k": nrm((nB, H, N), 0.1),
        "rw_ln_w": 1.0 + nrm((nB, D), 0.05),
        "rw_ln_b": nrm((nB, D), 0.02),
        "ffn_w_gate": nrm((DEPTH, D, F), D ** -0.5),
        "ffn_w_up": nrm((DEPTH, D, F), D ** -0.5),
        "ffn_conv_w": nrm((DEPTH, CONV_W, F), CONV_W ** -0.5),
        "ffn_conv_b": nrm((DEPTH, F), 0.02),
        "ffn_w_down": nrm((DEPTH, F, D), F ** -0.5),
    }

def reference(x_prompt, x_sample, norm_mix, norm_ffn, na_w_qkv, na_w_o, na_q_gain, na_k_gain, na_rpb,
              rw_mu, rw_w_r, rw_w_k, rw_w_v, rw_w_o, rw_w0, rw_w1, rw_w2, rw_a0, rw_a1, rw_a2,
              rw_v0, rw_v1, rw_v2, rw_g1, rw_g2, rw_k_k, rw_k_a, rw_r_k, rw_ln_w, rw_ln_b,
              ffn_w_gate, ffn_w_up, ffn_conv_w, ffn_conv_b, ffn_w_down):
    weights = (norm_mix, norm_ffn, na_w_qkv, na_w_o, na_q_gain, na_k_gain, na_rpb,
               rw_mu, rw_w_r, rw_w_k, rw_w_v, rw_w_o, rw_w0, rw_w1, rw_w2, rw_a0, rw_a1, rw_a2,
               rw_v0, rw_v1, rw_v2, rw_g1, rw_g2, rw_k_k, rw_k_a, rw_r_k, rw_ln_w, rw_ln_b,
               ffn_w_gate, ffn_w_up, ffn_conv_w, ffn_conv_b, ffn_w_down)
    y_prompt = _trunk(x_prompt, *weights)
    y_sample = _trunk(x_sample, *weights)
    return (y_prompt, y_sample)


_drawn_inputs = setup_inputs


def setup_inputs(seed=0):
    import zlib

    import numpy as np

    out = dict(_drawn_inputs(seed))
    spreads = {}
    factors = {'na_q_gain': 3.598,
     'na_k_gain': 3.886,
     'rw_w1': 5.432,
     'rw_w2': 5.386,
     'rw_a0': 3.195,
     'rw_ln_b': 6.621,
     'ffn_conv_b': 3.642,
     'rw_k_k': 5.62,
     'rw_k_a': 2.687,
     'rw_ln_w': 3.267}
    for name, (base, spread) in spreads.items():
        noise = np.random.default_rng([zlib.crc32(name.encode()), seed]).standard_normal(out[name].shape)
        drawn = base * np.exp(spread * noise) if base else spread * noise
        out[name] = __import__('jax').numpy.asarray(drawn.astype(out[name].dtype))
    for name, factor in factors.items():
        out[name] = (out[name] * factor).astype(out[name].dtype)
    return out
```

```python
from contextlib import ExitStack

import concourse.bass as bass
from concourse import mybir

F32 = mybir.dt.float32
F32R = mybir.dt.float32r
ALU = mybir.AluOpType
ACT = mybir.ActivationFunctionType
AX_X = mybir.AxisListType.X

P = 128
D = 1024
KT = D // P
T_PROMPT, T_SAMPLE = 1024, 256
T = T_PROMPT + T_SAMPLE
HEADS, HD = 16, 64
PAIRS = HEADS // 2
FF = 2816
FT = FF // P
GRID_W = 64
WIN_H, WIN_W = 8, 16
RPB_H, RPB_W = 2 * WIN_H - 1, 2 * WIN_W - 1
RMS_EPS = 1e-6
GN_EPS = 64e-5
NEG = -1e30
PADW = 2 * GRID_W - 1
TOK_GROUPS = ((0, 512), (512, 512), (1024, 256))
CREDIT = 2



class Phase:

    def __init__(self, nc, name):
        self.nc, self.name, self.ctx, self.own = nc, name, ExitStack(), []

    def __enter__(self):
        return self

    def __exit__(self, *a):
        if self.own and a[0] is None:
            self.nc.clear_and_free_semaphores(self.own)
            self.nc.all_engine_barrier()
        return self.ctx.__exit__(*a)

    def sb(self, name, shape, dt=F32):
        return self.ctx.enter_context(self.nc.sbuf_tensor(f"{self.name}_{name}", shape, dt))

    def ps(self, name, shape):
        return self.ctx.enter_context(self.nc.psum_tensor(f"{self.name}_{name}", shape, F32))

    def sem(self, name):
        self.own.append(self.nc.alloc_semaphore(f"{self.name}_{name}"))
        return self.own[-1]

    def sems(self, name, n):
        return [self.sem(f"{name}{i}") for i in range(n)]


def product_tile(nc, banks, wh, wl, xh, xl, kt):
    for k in range(kt):
        for w, xs in ((wh, (xh, xl)), (wl, (xh,))):
            for x in xs:
                for g, (t0, n) in enumerate(TOK_GROUPS):
                    last = nc.tensor.matmul(banks[:, g, 0:n], w[:, k, :], x[:, k, t0:t0 + n],
                                            start=(k == 0 and w is wh and x is xh),
                                            stop=(k == kt - 1 and w is wl))
    return last


def loop_peeled(eng, n, body, step=1):
    assert n % step == 0
    rounds = n // step
    if rounds > 1:
        with eng.Fori(0, rounds - 1) as j:
            for s in range(step):
                body(j * step + s, s, False)
    for s in range(step):
        body((rounds - 1) * step + s, s, s == step - 1)


def col(w, i, n=P):
    return w[:, bass.ds(i * n, n)]



def transpose_in(nc, x, xres, consts):
    with Phase(nc, "tin") as ph:
        ident = ph.sb("ident", [P, P])
        rows = ph.sb("rows", [P, 2, D])
        cols = ph.sb("cols", [P, 2, KT, P])
        ps = ph.ps("ps", [P, 2, KT, P])
        ident_in, rows_in, stored = ph.sem("ident_in"), ph.sems("rows_in", 2), ph.sems("stored", 2)
        turned, copied = ph.sem("turned"), ph.sem("copied")
        with nc.Block() as block:
            @block.sync
            def _(sp):
                sp.dma_start(ident[:], consts["ident"]).then_inc(ident_in, 16)
                sp.sem_inc(turned, CREDIT)
                with sp.Fori(0, T // P // 2) as j:
                    for s in range(2):
                        sp.wait_ge(turned, j * 2 + (s + 1))
                        sp.dma_start(rows[:, s, :], x[bass.ds(j * 2 * P + s * P, P), :]).then_inc(rows_in[s], 16)

            @block.tensor
            def _(pe):
                pe.wait_ge(ident_in, 16)
                pe.sem_inc(copied, CREDIT)
                with pe.Fori(0, T // P // 2) as j:
                    for s in range(2):
                        pe.wait_ge(rows_in[s], j * 16 + 16)
                        pe.wait_ge(copied, j * 2 + (s + 1))
                        for k in range(KT):
                            last = nc.tensor.transpose(ps[:, s, k, :], rows[:, s, k * P:(k + 1) * P], ident[:])
                        last.then_inc(turned, 1)

            @block.vector
            def _(dve):
                for s in range(2):
                    dve.sem_inc(stored[s], 16)
                with dve.Fori(0, T // P // 2) as j:
                    for s in range(2):
                        dve.wait_ge(turned, j * 2 + (s + 1 + CREDIT))
                        dve.wait_ge(stored[s], j * 16 + 16)
                        nc.vector.tensor_copy(cols[:, s], ps[:, s]).then_inc(copied, 1)

            @block.scalar
            def _(act):
                with act.Fori(0, T // P // 2) as j:
                    for s in range(2):
                        act.wait_ge(copied, j * 2 + (s + 1 + CREDIT))
                        act.dma_start(xres[:, :, bass.ds(j * 2 * P + s * P, P)], cols[:, s]).then_inc(stored[s], 16)
                for s in range(2):
                    act.wait_ge(stored[s], 16 * (T // P // 2) + 16)


def transpose_out(nc, xres, y, consts):
    with Phase(nc, "tout") as ph:
        ident = ph.sb("ident", [P, P])
        cols = ph.sb("cols", [P, 2, KT, P])
        rows = ph.sb("rows", [P, 2, KT, P])
        ps = ph.ps("ps", [P, 2, KT, P])
        ident_in, cols_in, stored = ph.sem("ident_in"), ph.sems("cols_in", 2), ph.sems("stored", 2)
        turned, copied = ph.sem("turned"), ph.sem("copied")
        with nc.Block() as block:
            @block.sync
            def _(sp):
                sp.dma_start(ident[:], consts["ident"]).then_inc(ident_in, 16)
                sp.sem_inc(turned, CREDIT)
                with sp.Fori(0, T // P // 2) as j:
                    for s in range(2):
                        sp.wait_ge(turned, j * 2 + (s + 1))
                        sp.dma_start(cols[:, s], xres[:, :, bass.ds(j * 2 * P + s * P, P)]).then_inc(cols_in[s], 16)

            @block.tensor
            def _(pe):
                pe.wait_ge(ident_in, 16)
                pe.sem_inc(copied, CREDIT)
                with pe.Fori(0, T // P // 2) as j:
                    for s in range(2):
                        pe.wait_ge(cols_in[s], j * 16 + 16)
                        pe.wait_ge(copied, j * 2 + (s + 1))
                        for k in range(KT):
                            last = nc.tensor.transpose(ps[:, s, k, :], cols[:, s, k, :], ident[:])
                        last.then_inc(turned, 1)

            @block.vector
            def _(dve):
                for s in range(2):
                    dve.sem_inc(stored[s], 16)
                with dve.Fori(0, T // P // 2) as j:
                    for s in range(2):
                        dve.wait_ge(turned, j * 2 + (s + 1 + CREDIT))
                        dve.wait_ge(stored[s], j * 16 + 16)
                        nc.vector.tensor_copy(rows[:, s], ps[:, s]).then_inc(copied, 1)

            @block.scalar
            def _(act):
                with act.Fori(0, T // P // 2) as j:
                    for s in range(2):
                        act.wait_ge(copied, j * 2 + (s + 1 + CREDIT))
                        act.dma_start(y[bass.ds(j * 2 * P + s * P, P), :],
                                      rows[:, s].rearrange("p k f -> p (k f)")).then_inc(stored[s], 16)
                for s in range(2):
                    act.wait_ge(stored[s], 16 * (T // P // 2) + 16)



def rms_norm(nc, name, xres, gain, consts, out_hi, out_lo):
    with Phase(nc, name) as ph:
        xt = ph.sb("xt", [P, KT, T])
        sq = ph.sb("sq", [P, 2, T])
        rs = ph.sb("rs", [P, T])
        h = ph.sb("h", [P, 2, T])
        g = ph.sb("g", [P, KT])
        ones = ph.sb("ones", [P, P])
        ps = ph.ps("ps", [P, 3, 512])
        small_in, x_in = ph.sem("small_in"), ph.sems("x_in", KT)
        squared, summed, rs_done = ph.sem("squared"), ph.sem("summed"), ph.sem("rs_done")
        h_done, hi_done, lo_done = ph.sem("h_done"), ph.sem("hi_done"), ph.sem("lo_done")
        with nc.Block() as block:
            @block.sync
            def _(sp):
                sp.dma_start(ones[:], consts["ones"]).then_inc(small_in, 16)
                for k in range(KT):
                    sp.dma_start(xt[:, k, :], xres[:, k, :]).then_inc(x_in[k], 16)
                with nc.allow_non_contiguous_dma("gain by channel"):
                    sp.dma_start(g[:], gain.rearrange("(k p) -> p k", p=P)).then_inc(small_in, 16)

            @block.scalar
            def _(act):
                for k in range(KT):
                    act.wait_ge(x_in[k], 16)
                    if k >= 2:
                        act.wait_ge(summed, k - 1)
                    nc.scalar.activation(sq[:, k % 2], xt[:, k], ACT.Square).then_inc(squared, 1)
                act.wait_ge(rs_done, 1)
                nc.scalar.activation(rs[:], rs[:], ACT.Sqrt).then_inc(rs_done, 1)
                if out_lo is not None:
                    for k in range(KT):
                        act.wait_ge(h_done, k + 1)
                        nc.scalar.activation(out_hi[:, k], h[:, k % 2], ACT.Copy).then_inc(hi_done, 1)

            @block.tensor
            def _(pe):
                pe.wait_ge(small_in, 32)
                for k in range(KT):
                    pe.wait_ge(squared, k + 1)
                    for gi, (t0, n) in enumerate(TOK_GROUPS):
                        last = nc.tensor.matmul(ps[:, gi, 0:n], ones[:], sq[:, k % 2, t0:t0 + n],
                                                start=(k == 0), stop=(k == KT - 1))
                    last.then_inc(summed, 1)

            @block.vector
            def _(dve):
                dve.wait_ge(summed, KT)
                for gi, (t0, n) in enumerate(TOK_GROUPS):
                    last = nc.vector.tensor_scalar(rs[:, t0:t0 + n], ps[:, gi, 0:n], 1.0 / D, RMS_EPS,
                                                   ALU.mult, ALU.add)
                last.then_inc(rs_done, 1)
                dve.wait_ge(rs_done, 2)
                nc.vector.reciprocal(rs[:], rs[:]).then_inc(rs_done, 1)
                dve.wait_ge(rs_done, 3)
                dve.wait_ge(small_in, 32)
                for k in range(KT):
                    if out_lo is None:
                        nc.vector.scalar_tensor_tensor(out_hi[:, k], xt[:, k], g[:, k:k + 1], rs[:],
                                                       ALU.mult, ALU.mult)
                        continue
                    if k >= 2:
                        dve.wait_ge(lo_done, k - 1)
                    nc.vector.scalar_tensor_tensor(h[:, k % 2], xt[:, k], g[:, k:k + 1], rs[:],
                                                   ALU.mult, ALU.mult).then_inc(h_done, 1)

            @block.gpsimd
            def _(pool):
                if out_lo is not None:
                    for k in range(KT):
                        pool.wait_ge(hi_done, k + 1)
                        nc.gpsimd.tensor_tensor(out_lo[:, k], h[:, k % 2], out_hi[:, k].bitcast(F32),
                                                ALU.subtract).then_inc(lo_done, 1)



def residual_product(nc, name, w, kt, xh, xl, xres):
    wv = w.rearrange("(k p) n -> p k n", p=P)
    with Phase(nc, name) as ph:
        raw = ph.sb("raw", [P, 2, kt, P])
        wh = ph.sb("wh", [P, 2, kt, P], F32R)
        wl = ph.sb("wl", [P, 2, kt, P], F32R)
        xo = ph.sb("xo", [P, 2, T])
        ps = ph.ps("ps", [P, 2, 3, 512])
        w_in, x_in, stored = ph.sems("w_in", 2), ph.sems("x_in", 2), ph.sems("stored", 2)
        hi_done, lo_done, prod_done, added = (ph.sem(n) for n in ("hi_done", "lo_done", "prod_done", "added"))
        with nc.Block() as block:
            @block.sync
            def _(sp):
                sp.sem_inc(lo_done, CREDIT)
                for s in range(2):
                    sp.sem_inc(stored[s], 16)

                def load(i, s, r):
                    sp.wait_ge(lo_done, i + 1)
                    sp.dma_start(raw[:, s], wv[:, :, bass.ds(i * P, P)]).then_inc(w_in[s], 16)
                    sp.wait_ge(stored[s], r * 16 + 16)
                    sp.dma_start(xo[:, s], xres[:, bass.ds(i, 1), :].rearrange("p a t -> p (a t)")).then_inc(x_in[s], 16)

                load(0, 0, 0)

                def store(i, s):
                    sp.wait_ge(added, i + (1 + CREDIT))
                    sp.dma_start(xres[:, bass.ds(i, 1), :].rearrange("p a t -> p (a t)"), xo[:, s]).then_inc(stored[s], 16)

                with sp.Fori(0, KT // 2 - 1) as j:
                    load(j * 2 + 1, 1, j)
                    store(j * 2, 0)
                    load(j * 2 + 2, 0, j + 1)
                    store(j * 2 + 1, 1)
                load(KT - 1, 1, KT // 2 - 1)
                store(KT - 2, 0)
                store(KT - 1, 1)
                for s in range(2):
                    sp.wait_ge(stored[s], 16 * (KT // 2) + 16)

            @block.scalar
            def _(act):
                act.sem_inc(prod_done, CREDIT)
                with act.Fori(0, KT // 2) as j:
                    for s in range(2):
                        act.wait_ge(w_in[s], j * 16 + 16)
                        act.wait_ge(prod_done, j * 2 + (s + 1))
                        nc.scalar.activation(wh[:, s], raw[:, s], ACT.Copy).then_inc(hi_done, 1)

            @block.gpsimd
            def _(pool):
                with pool.Fori(0, KT // 2) as j:
                    for s in range(2):
                        pool.wait_ge(hi_done, j * 2 + (s + 1))
                        nc.gpsimd.tensor_tensor(wl[:, s], raw[:, s], wh[:, s].bitcast(F32),
                                                ALU.subtract).then_inc(lo_done, 1)

            @block.tensor
            def _(pe):
                pe.sem_inc(added, CREDIT)
                with pe.Fori(0, KT // 2) as j:
                    for s in range(2):
                        pe.wait_ge(lo_done, j * 2 + (s + 1 + CREDIT))
                        pe.wait_ge(added, j * 2 + (s + 1))
                        product_tile(nc, ps[:, s], wh[:, s], wl[:, s], xh, xl, kt).then_inc(prod_done, 1)

            @block.vector
            def _(dve):
                with dve.Fori(0, KT // 2) as j:
                    for s in range(2):
                        dve.wait_ge(prod_done, j * 2 + (s + 1 + CREDIT))
                        dve.wait_ge(x_in[s], j * 16 + 16)
                        for g, (t0, n) in enumerate(TOK_GROUPS):
                            last = nc.vector.tensor_tensor(xo[:, s, t0:t0 + n], ps[:, s, g, 0:n],
                                                           xo[:, s, t0:t0 + n], ALU.add)
                        last.then_inc(added, 1)



GP_W = T + 3


def ffn_up(nc, name, w_gate, w_up, conv_w, conv_b, f0, nf, hh, hl, ah, al):
    gv = w_gate.rearrange("(k p) n -> p k n", p=P)
    uv = w_up.rearrange("(k p) n -> p k n", p=P)
    with Phase(nc, name) as ph:
        raw = ph.sb("raw", [P, 2, KT, P])
        wh = ph.sb("wh", [P, 2, KT, P], F32R)
        wl = ph.sb("wl", [P, 2, KT, P], F32R)
        gp = ph.sb("gp", [P, GP_W])
        cv = ph.sb("cv", [P, T + 1])
        cw = ph.sb("cw", [P, 4, nf])
        ps = ph.ps("ps", [P, 2, 3, 512])
        w_in, cw_in = ph.sems("w_in", 2), ph.sem("cw_in")
        hi_done, lo_done = ph.sems("hi_done", 2), ph.sems("lo_done", 2)
        prod, gate_out, zeroed = ph.sems("prod", 2), ph.sem("gate_out"), ph.sem("zeroed")
        conv_step, conv_done, silu_done, mul_done, act_hi, act_lo = (
            ph.sem(n) for n in ("conv_step", "conv_done", "silu_done", "mul_done", "act_hi", "act_lo"))
        with nc.Block() as block:
            @block.sync
            def _(sp):
                with nc.allow_non_contiguous_dma("convolution weights by channel"):
                    for c in range(3):
                        sp.dma_start(cw[:, c], conv_w[c, f0 * P:(f0 + nf) * P].rearrange("(f p) -> p f", p=P)).then_inc(cw_in, 16)
                    sp.dma_start(cw[:, 3], conv_b[f0 * P:(f0 + nf) * P].rearrange("(f p) -> p f", p=P)).then_inc(cw_in, 16)
                for s in range(2):
                    sp.sem_inc(lo_done[s], 1)
                with sp.Fori(0, nf) as i:
                    for s, wv in enumerate((gv, uv)):
                        sp.wait_ge(lo_done[s], i + 1)
                        sp.dma_start(raw[:, s], wv[:, :, bass.ds(i * P + f0 * P, P)]).then_inc(w_in[s], 16)

            @block.gpsimd
            def _(pool):
                nc.gpsimd.memset(gp[:], 0.0).then_inc(zeroed, 1)
                with pool.Fori(0, nf) as i:
                    for s in range(2):
                        pool.wait_ge(hi_done[s], i + 1)
                        nc.gpsimd.tensor_tensor(wl[:, s], raw[:, s], wh[:, s].bitcast(F32),
                                                ALU.subtract).then_inc(lo_done[s], 1)

            @block.tensor
            def _(pe):
                pe.sem_inc(gate_out, 1)
                pe.sem_inc(mul_done, 1)
                with pe.Fori(0, nf) as i:
                    pe.wait_ge(lo_done[0], i + 2)
                    pe.wait_ge(gate_out, i + 1)
                    product_tile(nc, ps[:, 0], wh[:, 0], wl[:, 0], hh, hl, KT).then_inc(prod[0], 1)
                    pe.wait_ge(lo_done[1], i + 2)
                    pe.wait_ge(mul_done, i + 1)
                    product_tile(nc, ps[:, 1], wh[:, 1], wl[:, 1], hh, hl, KT).then_inc(prod[1], 1)

            @block.scalar
            def _(act):
                for s in range(2):
                    act.sem_inc(prod[s], 1)
                act.sem_inc(conv_done, 1)
                act.wait_ge(zeroed, 1)

                def cut(i, s):
                    act.wait_ge(w_in[s], i * 16 + 16)
                    act.wait_ge(prod[s], i + 1)
                    nc.scalar.activation(wh[:, s], raw[:, s], ACT.Copy).then_inc(hi_done[s], 1)

                def body(i, s, last):
                    cut(i, 1)
                    act.wait_ge(prod[0], i + 2)
                    act.wait_ge(conv_done, i + 1)
                    nc.scalar.activation(gp[:, 1:1025], ps[:, 0, 0:2, :].rearrange("p g n -> p (g n)"), ACT.Copy)
                    nc.scalar.activation(gp[:, 1026:1282], ps[:, 0, 2, 0:256], ACT.Copy).then_inc(gate_out, 1)
                    if not last:
                        cut(i + 1, 0)
                    act.wait_ge(conv_done, i + 2)
                    nc.scalar.activation(cv[:], cv[:], ACT.Silu, bias=cw[:, 3, bass.ds(i, 1)]).then_inc(silu_done, 1)
                    act.wait_ge(mul_done, i + 2)
                    nc.scalar.activation(ah[:, bass.ds(i, 1), 0:1024].rearrange("p a t -> p (a t)"), cv[:, 0:1024], ACT.Copy)
                    nc.scalar.activation(ah[:, bass.ds(i, 1), 1024:1280].rearrange("p a t -> p (a t)"), cv[:, 1025:1281],
                                         ACT.Copy).then_inc(act_hi, 1)

                cut(0, 0)
                loop_peeled(act, nf, body)

            @block.vector
            def _(dve):
                dve.wait_ge(cw_in, 64)
                dve.sem_inc(conv_step, 1)
                with dve.Fori(0, nf) as i:
                    dve.wait_ge(gate_out, i + 2)
                    c = lambda x: cw[:, x, bass.ds(i, 1)]
                    nc.vector.tensor_scalar(cv[:], gp[:, 0:T + 1], c(0), None, ALU.mult).then_inc(conv_step, 1)
                    dve.wait_ge(conv_step, i * 2 + 2)
                    nc.vector.scalar_tensor_tensor(cv[:], gp[:, 1:T + 2], c(1), cv[:], ALU.mult, ALU.add).then_inc(conv_step, 1)
                    dve.wait_ge(conv_step, i * 2 + 3)
                    nc.vector.scalar_tensor_tensor(cv[:], gp[:, 2:T + 3], c(2), cv[:], ALU.mult, ALU.add).then_inc(conv_done, 1)
                    dve.wait_ge(silu_done, i + 1)
                    dve.wait_ge(prod[1], i + 2)
                    nc.vector.tensor_tensor(cv[:, 0:1024], ps[:, 1, 0:2, :].rearrange("p g n -> p (g n)"), cv[:, 0:1024], ALU.mult)
                    nc.vector.tensor_tensor(cv[:, 1025:1281], ps[:, 1, 2, 0:256], cv[:, 1025:1281], ALU.mult).then_inc(mul_done, 1)
                    dve.wait_ge(act_hi, i + 1)
                    nc.vector.tensor_tensor(al[:, bass.ds(i, 1), 0:1024].rearrange("p a t -> p (a t)"), cv[:, 0:1024],
                                            ah[:, bass.ds(i, 1), 0:1024].bitcast(F32).rearrange("p a t -> p (a t)"), ALU.subtract)
                    nc.vector.tensor_tensor(al[:, bass.ds(i, 1), 1024:1280].rearrange("p a t -> p (a t)"), cv[:, 1025:1281],
                                            ah[:, bass.ds(i, 1), 1024:1280].bitcast(F32).rearrange("p a t -> p (a t)"),
                                            ALU.subtract).then_inc(act_lo, 1)
                    dve.wait_ge(act_lo, i + 1)


def ffn(nc, name, xres, gain, w_gate, w_up, conv_w, conv_b, w_down, consts):
    with Phase(nc, name) as ph:
        hh = ph.sb("hh", [P, KT, T], F32R)
        hl = ph.sb("hl", [P, KT, T], F32R)
        rms_norm(nc, name + "n", xres, gain, consts, hh, hl)
        for f0, nf in ((0, 8), (8, 7), (15, 7)):
            with Phase(nc, f"{name}g{f0}") as gph:
                ah = gph.sb("ah", [P, nf, T], F32R)
                al = gph.sb("al", [P, nf, T], F32R)
                ffn_up(nc, f"{name}u{f0}", w_gate, w_up, conv_w, conv_b, f0, nf, hh, hl, ah, al)
                residual_product(nc, f"{name}d{f0}", w_down[f0 * P:(f0 + nf) * P, :], nf, ah, al, xres)



BT_U = 14
BI_U = 9
UMAX = BI_U * GRID_W


def query_tiles():
    out = []
    for base, rows in ((0, T_PROMPT // GRID_W), (T_PROMPT, T_SAMPLE // GRID_W)):
        kh = min(WIN_H, rows)
        for r in range(0, rows, 2):
            lo = [min(max(q - kh // 2, 0), rows - kh) for q in (r, r + 1)]
            inner = lo[0] != lo[1]
            first, n = lo[0], lo[1] + kh - lo[0]
            u = first - r + WIN_H - 1
            assert not inner or (u == 3 and n == BI_U)
            assert first % 2 == 0 and u >= 1 and u + n <= 15
            out.append((base + r * GRID_W, base + first * GRID_W, n * GRID_W, inner, 0 if inner else u - 1))
    return out


def lay_out_bias(nc, rpb, padded, shifted_bias):
    pad0 = (PADW - RPB_W) // 2
    with Phase(nc, "pad") as ph:
        zeros = ph.sb("zeros", [2 * RPB_H, PADW])
        zeroed, cleared, filled, spread = (ph.sem(n) for n in ("zeroed", "cleared", "filled", "spread"))
        with nc.Block() as block:
            @block.vector
            def _(dve):
                nc.vector.memset(zeros[:], 0.0).then_inc(zeroed, 1)

            @block.sync
            def _(sp):
                sp.wait_ge(zeroed, 1)
                for a in range(PAIRS):
                    sp.dma_start(padded[a].rearrange("h r c -> (h r) c"), zeros[:]).then_inc(cleared, 16)
                sp.wait_ge(cleared, 16 * PAIRS)
                for a in range(PAIRS):
                    sp.dma_start(padded[a, :, :, pad0:pad0 + RPB_W], rpb[2 * a:2 * a + 2]).then_inc(filled, 16)
                sp.wait_ge(filled, 16 * PAIRS)
                for a in range(PAIRS):
                    for head in range(2):
                        one = padded[a, head]
                        src = bass.AP(tensor=one.tensor, offset=one.offset + (GRID_W - 1),
                                      ap=[[PADW, RPB_H], [-1, GRID_W], [1, GRID_W]])
                        sp.dma_start(shifted_bias[a, head], src).then_inc(spread, 16)
                sp.wait_ge(spread, 32 * PAIRS)


def attention(nc, w_qkv, q_gain, k_gain, shifted_bias, hh, hl, o, consts):
    wv = w_qkv.rearrange("(k p) n -> p k n", p=P)
    tiles = query_tiles()
    NT = len(tiles)
    NU = 2 * NT
    with Phase(nc, "att") as ph:
        raw = ph.sb("raw", [P, 2, KT, P])
        wh = ph.sb("wh", [P, 3, KT, P], F32R)
        wl = ph.sb("wl", [P, 3, KT, P], F32R)
        qk = ph.sb("qk", [P, 2, T])
        sq = ph.sb("sq", [P, T])
        v = ph.sb("v", [P, T // P, P])
        bt = ph.sb("bt", [P, 2, BT_U, GRID_W])
        bi = ph.sb("bi", [P, 2, BI_U, GRID_W])
        e = ph.sb("e", [P, 2, UMAX])
        et = ph.sb("et", [P, 2, 5, P])
        otok = ph.sb("otok", [P, 2, P])
        stat = ph.sb("stat", [P, 2, 4])
        gains = ph.sb("gains", [P, 2])
        mask = ph.sb("mask", [P, 2, GRID_W])
        ident = ph.sb("ident", [P, P])
        block64 = ph.sb("block64", [P, P])
        proj = ph.ps("proj", [P, 3, 512])
        score = ph.ps("score", [P, 2, 1024])
        misc = ph.ps("misc", [P, 512])
        turn = (proj[:, 0], proj[:, 1])
        out_rows = proj[:, 2]
        small_in, w_in, bias_in = ph.sem("small_in"), ph.sems("w_in", 2), ph.sem("bias_in")
        cut_hi, cut_lo = ph.sem("cut_hi"), ph.sem("cut_lo")
        projected, proj_out, squared, summed, root, normed = (
            ph.sem(n) for n in ("projected", "proj_out", "squared", "summed", "root", "normed"))
        rs_steps, biased = ph.sem("rs_steps"), ph.sem("biased")
        scored, shifted, maxed, exped = (ph.sem(n) for n in ("scored", "shifted", "maxed", "exped"))
        turned, turn_out, summed_v, o_rows, o_turned, o_done, inv = (
            ph.sem(n) for n in ("turned", "turn_out", "summed_v", "o_rows", "o_turned", "o_done", "inv"))
        pair_done = ph.sem("pair_done")
        chain = ph.sem("chain")
        held = ph.sem("held")
        with nc.Block() as block:
            @block.sync
            def _(sp):
                sp.dma_start(ident[:], consts["ident"]).then_inc(small_in, 16)
                sp.dma_start(block64[:], consts["block64"]).then_inc(small_in, 16)
                sp.dma_start(mask[:], consts["colmask"]).then_inc(small_in, 16)
                with nc.allow_non_contiguous_dma("gains by channel"):
                    for half in range(2):
                        for n, gain in enumerate((q_gain, k_gain)):
                            sp.dma_start(gains[half * HD:(half + 1) * HD, n:n + 1],
                                         gain.rearrange("(p a) -> p a", a=1)).then_inc(small_in, 16)
                sp.sem_inc(cut_lo, CREDIT)
                sp.sem_inc(pair_done, 1)
                with sp.Fori(0, PAIRS) as p:
                    sp.wait_ge(pair_done, p + 1)
                    for half in range(2):
                        for head in range(2):
                            src = shifted_bias[bass.ds(p, 1), head, 1 - half:1 - half + BT_U].rearrange("a r c k -> c (a r) k")
                            sp.dma_start(bt[half * HD:(half + 1) * HD, head], src).then_inc(bias_in, 16)
                    for c in range(3):
                        sp.wait_ge(cut_lo, p * 3 + (c + 1))
                        if c < 2:
                            sp.dma_start(raw[:, c], wv[:, :, bass.ds(p * P + c * D, P)]).then_inc(w_in[c], 16)
                        else:
                            sp.dma_start(raw[:, 0], wv[:, :, bass.ds(p * P + c * D, P)]).then_inc(w_in[0], 16)

            @block.gpsimd
            def _(pool):
                nc.gpsimd.memset(bi[:], NEG).then_inc(biased, 1)
                pool.wait_ge(small_in, 16 * 7)
                with pool.Fori(0, PAIRS) as p:
                    for c in range(3):
                        pool.wait_ge(cut_hi, p * 3 + (c + 1))
                        nc.gpsimd.tensor_tensor(wl[:, c], raw[:, c % 2], wh[:, c].bitcast(F32),
                                                ALU.subtract).then_inc(cut_lo, 1)

            @block.scalar
            def _(act):
                act.wait_ge(small_in, 16 * 7)
                act.sem_inc(projected, 3)
                with act.Fori(0, PAIRS) as p:
                    for c in range(3):
                        act.wait_ge(w_in[c % 2], p * 16 + 16 if c == 1 else p * 32 + 16 * (1 + c // 2))
                        act.wait_ge(projected, p * 3 + (c + 1))
                        nc.scalar.activation(wh[:, c], raw[:, c % 2], ACT.Copy).then_inc(cut_hi, 1)
                    for c in range(2):
                        act.wait_ge(projected, p * 3 + (c + 1 + 3))
                        act.wait_ge(pair_done, p + 1)
                        nc.scalar.activation(qk[:, c, 0:1024], proj[:, 0:2, :].rearrange("p g n -> p (g n)"), ACT.Copy)
                        nc.scalar.activation(qk[:, c, 1024:1280], proj[:, 2, 0:256], ACT.Copy).then_inc(proj_out, 1)
                        act.wait_ge(proj_out, p * 3 + (c + 1))
                        if c:
                            act.wait_ge(normed, p * 2 + 1)
                        nc.scalar.activation(sq[:], qk[:, c], ACT.Square).then_inc(squared, 1)
                        act.wait_ge(rs_steps, p * 4 + (c * 2 + 1))
                        nc.scalar.activation(sq[:], sq[:], ACT.Sqrt).then_inc(root, 1)
                    act.wait_ge(projected, p * 3 + 6)
                    nc.scalar.activation(v[:, 0:8].rearrange("p a n -> p (a n)"), proj[:, 0:2, :].rearrange("p g n -> p (g n)"), ACT.Copy)
                    nc.scalar.activation(v[:, 8:10].rearrange("p a n -> p (a n)"), proj[:, 2, 0:256], ACT.Copy).then_inc(proj_out, 1)
                    for u in range(NU + 1):
                        if u < NU:
                            q0, k0, nk, inner, off = tiles[u // 2]
                            s = u % 2
                            act.wait_ge(maxed, p * NU + (u + 1))
                            nc.scalar.activation(e[:, s, 0:nk], e[:, s, 0:nk], ACT.Exp, bias=stat[:, s, 1:2],
                                                 accum_out=stat[:, s, 2:3]).then_inc(exped, 1)
                        if u >= 1:
                            w = u - 1
                            nk = tiles[w // 2][2]
                            s = w % 2
                            act.wait_ge(turned, p * NU + (w + 1))
                            if w >= 2:
                                act.wait_ge(summed_v, p * NU + (w - 1))
                            nb = min(nk, 512)
                            last = nc.scalar.activation(et[:, s, 0:nb // P].rearrange("p a n -> p (a n)"), turn[s][:, 0:nb], ACT.Copy)
                            if nk > 512:
                                last = nc.scalar.activation(et[0:GRID_W, s, 4], misc[0:GRID_W, 0:P], ACT.Copy)
                            last.then_inc(turn_out, 1)
                            if w % 2 == 0 and w >= 2:
                                t = w // 2 - 1
                                act.wait_ge(o_turned, p * NT + (t + 1))
                                nc.scalar.activation(o[:, bass.ds(p, 1), tiles[t][0]:tiles[t][0] + P].rearrange("p a t -> p (a t)"),
                                                     misc[:, P:2 * P], ACT.Copy).then_inc(o_done, 1)
                    act.wait_ge(o_turned, p * NT + NT)
                    t = NT - 1
                    nc.scalar.activation(o[:, bass.ds(p, 1), tiles[t][0]:tiles[t][0] + P].rearrange("p a t -> p (a t)"),
                                         misc[:, P:2 * P], ACT.Copy).then_inc(pair_done, 1)

            @block.tensor
            def _(pe):
                pe.wait_ge(small_in, 16 * 7)
                with pe.Fori(0, PAIRS) as p:
                    pe.wait_ge(pair_done, p + 1)
                    for c in range(2):
                        pe.wait_ge(cut_lo, p * 3 + (c + 1 + CREDIT))
                        if c:
                            pe.wait_ge(rs_steps, p * 4 + 1)
                        product_tile(nc, proj, wh[:, c], wl[:, c], hh, hl, KT).then_inc(projected, 1)
                        pe.wait_ge(squared, p * 2 + (c + 1))
                        for g, (t0, n) in enumerate(TOK_GROUPS):
                            last = nc.tensor.matmul(proj[:, g, 0:n], block64[:], sq[:, t0:t0 + n], start=True, stop=True)
                        last.then_inc(summed, 1)
                    pe.wait_ge(cut_lo, p * 3 + (3 + CREDIT))
                    pe.wait_ge(rs_steps, p * 4 + 3)
                    for t in range(T // P):
                        bank = proj[:, t // 4, (t % 4) * P:(t % 4 + 1) * P]
                        for k in range(KT):
                            for x, w in ((hh, wh), (hh, wl), (hl, wh)):
                                last = nc.tensor.matmul(bank, x[:, k, t * P:(t + 1) * P], w[:, 2, k, :],
                                                        start=(k == 0 and x is hh and w is wh), stop=(k == KT - 1 and x is hl))
                    last.then_inc(projected, 1)

                    def scores(u):
                        q0, k0, nk, inner, off = tiles[u // 2]
                        s = u % 2
                        rows = slice(s * HD, (s + 1) * HD)
                        if u == 0:
                            pe.wait_ge(normed, p * 2 + 2)
                        if u >= 2:
                            pe.wait_ge(shifted, p * NU + (u - 1))
                        nb = min(nk, 512)
                        last = nc.tensor.matmul(score[:, s, 0:nb], qk[rows, 0, q0:q0 + P], qk[rows, 1, k0:k0 + nb],
                                                start=True, stop=True)
                        if nk > 512:
                            last = nc.tensor.matmul(score[:, s, 512:nk], qk[rows, 0, q0:q0 + P], qk[rows, 1, k0 + 512:k0 + nk],
                                                    start=True, stop=True)
                        last.then_inc(scored, 1)

                    def turn_rows(t):
                        pe.wait_ge(o_rows, p * NU + (2 * t + 2))
                        if t >= 1:
                            pe.wait_ge(o_done, p * (NT - 1) + t)
                        nc.tensor.transpose(misc[:, P:2 * P], otok[:, t % 2], ident[:]).then_inc(o_turned, 1)

                    scores(0)
                    scores(1)
                    for u in range(NU):
                        q0, k0, nk, inner, off = tiles[u // 2]
                        s = u % 2
                        pe.wait_ge(exped, p * NU + (u + 1))
                        if u == 0:
                            pe.wait_ge(proj_out, p * 3 + 3)
                        fifth = nk > 512
                        if u >= 2:
                            pe.wait_ge(turn_out, p * NU + (u if fifth else u - 1))
                        if fifth and u >= 3:
                            pe.wait_ge(o_done, p * (NT - 1) + (u - 1) // 2)
                        for b in range(min(nk, 512) // P):
                            last = nc.tensor.transpose(turn[s][:, b * P:(b + 1) * P], e[:, s, b * P:(b + 1) * P], ident[:])
                        if nk > 512:
                            last = nc.tensor.transpose(misc[0:GRID_W, 0:P], e[:, s, 512:nk], ident[:])
                        last.then_inc(turned, 1)
                        if u + 2 < NU:
                            scores(u + 2)
                        pe.wait_ge(turn_out, p * NU + (u + 1))
                        if u >= 1:
                            pe.wait_ge(o_rows, p * NU + u)
                        nb = -(-nk // P)
                        for b in range(nb):
                            rows = min(P, nk - b * P)
                            last = nc.tensor.matmul(out_rows[:, 0:HD], et[0:rows, s, b], v[0:rows, k0 // P + b, s * HD:(s + 1) * HD],
                                                    start=(b == 0), stop=(b == nb - 1))
                        last.then_inc(summed_v, 1)
                        if s == 0 and u >= 2:
                            turn_rows(u // 2 - 1)
                    turn_rows(NT - 1)

            @block.vector
            def _(dve):
                dve.wait_ge(small_in, 16 * 7)
                nc.vector.tensor_scalar(gains[:, 0:1], gains[:, 0:1], HD ** -0.5, None, ALU.mult).then_inc(chain, 1)
                dve.wait_ge(chain, 1)
                with dve.Fori(0, PAIRS) as p:
                    dve.wait_ge(bias_in, p * 64 + 64)
                    for head in range(2):
                        nc.vector.tensor_tensor(bt[:, head], bt[:, head], mask[:, 0:1, :].to_broadcast([P, BT_U, GRID_W]), ALU.mult).then_inc(biased, 1)
                    dve.wait_ge(biased, p * 4 + 3)
                    for head in range(2):
                        nc.vector.tensor_tensor(bt[:, head], bt[:, head], mask[:, 1:2, :].to_broadcast([P, BT_U, GRID_W]), ALU.add).then_inc(biased, 1)
                    dve.wait_ge(biased, p * 4 + 5)
                    for head in range(2):
                        nc.vector.tensor_copy(bi[0:HD, head, 0:8], bt[0:HD, head, 2:10]).then_inc(chain, 1)
                        nc.vector.tensor_copy(bi[HD:P, head, 1:9], bt[HD:P, head, 3:11]).then_inc(chain, 1)
                    for c in range(2):
                        dve.wait_ge(summed, p * 2 + (c + 1))
                        for g, (t0, n) in enumerate(TOK_GROUPS):
                            last = nc.vector.tensor_scalar(sq[:, t0:t0 + n], proj[:, g, 0:n], 1.0 / HD, RMS_EPS, ALU.mult, ALU.add)
                        last.then_inc(rs_steps, 1)
                        dve.wait_ge(root, p * 2 + (c + 1))
                        nc.vector.reciprocal(sq[:], sq[:]).then_inc(rs_steps, 1)
                        dve.wait_ge(rs_steps, p * 4 + (2 * c + 2))
                        nc.vector.scalar_tensor_tensor(qk[:, c], qk[:, c], gains[:, c:c + 1], sq[:], ALU.mult, ALU.mult).then_inc(normed, 1)
                        if c == 0:
                            dve.wait_ge(normed, p * 2 + 1)
                    dve.wait_ge(chain, p * 4 + 5)

                    def shift(u):
                        q0, k0, nk, inner, off = tiles[u // 2]
                        s = u % 2
                        dve.wait_ge(scored, p * NU + (u + 1))
                        if u >= 2:
                            dve.wait_ge(turned, p * NU + (u - 1))
                        dve.sem_inc(held, 1)
                        b = bi[:, s] if inner else bt[:, s, off:off + nk // GRID_W]
                        nc.vector.tensor_tensor_reduce(e[:, s, 0:nk], score[:, s, 0:nk], b.rearrange("p r c -> p (r c)"), 1.0, NEG,
                                                       ALU.add, ALU.max, stat[:, s, 0:1]).then_inc(shifted, 1)
                        dve.wait_ge(shifted, p * NU + (u + 1))
                        nc.vector.tensor_scalar(stat[:, s, 1:2], stat[:, s, 0:1], -1.0, None, ALU.mult).then_inc(maxed, 1)

                    shift(0)
                    shift(1)
                    for u in range(NU):
                        s = u % 2
                        dve.wait_ge(exped, p * NU + (u + 1))
                        nc.vector.reciprocal(stat[:, s, 3:4], stat[:, s, 2:3]).then_inc(inv, 1)
                        dve.wait_ge(inv, p * NU + (u + 1))
                        dve.wait_ge(summed_v, p * NU + (u + 1))
                        if u >= 4:
                            dve.wait_ge(o_turned, p * NT + (u // 2 - 1))
                        nc.vector.tensor_scalar(otok[:, (u // 2) % 2, s * HD:(s + 1) * HD], out_rows[:, 0:HD], stat[:, s, 3:4], None,
                                                ALU.mult).then_inc(o_rows, 1)
                        if u + 2 < NU:
                            shift(u + 2)


def cut_activations(nc, name, src, hi, lo):
    with Phase(nc, name) as ph:
        hi_done, lo_done = ph.sem("hi_done"), ph.sem("lo_done")
        with nc.Block() as block:
            @block.scalar
            def _(act):
                for k in range(KT):
                    nc.scalar.activation(hi[:, k], src[:, k], ACT.Copy).then_inc(hi_done, 1)

            @block.vector
            def _(dve):
                for k in range(KT):
                    dve.wait_ge(hi_done, k + 1)
                    nc.vector.tensor_tensor(lo[:, k], src[:, k], hi[:, k].bitcast(F32), ALU.subtract)


def attention_layer(nc, xres, gain, w_qkv, w_o, q_gain, k_gain, rpb, padded, shifted_bias, consts):
    with Phase(nc, "al") as ph:
        hh = ph.sb("hh", [P, KT, T], F32R)
        hl = ph.sb("hl", [P, KT, T], F32R)
        rms_norm(nc, "an", xres, gain, consts, hh, hl)
        with Phase(nc, "alo") as oph:
            o = oph.sb("o", [P, KT, T])
            lay_out_bias(nc, rpb, padded, shifted_bias)
            attention(nc, w_qkv, q_gain, k_gain, shifted_bias, hh, hl, o, consts)
            cut_activations(nc, "oc", o, hh, hl)
        residual_product(nc, "ao", w_o, KT, hh, hl, xres)



def mix_differences(nc, h, xx):
    with Phase(nc, "mx") as ph:
        step = ph.sem("step")
        with nc.Block() as block:
            @block.vector
            def _(dve):
                nc.vector.tensor_tensor(xx[:, :, 1:T - 1], h[:, :, 0:T - 2], h[:, :, 2:T], ALU.add).then_inc(step, 1)
                dve.wait_ge(step, 1)
                for at, neighbour in ((0, 1), (T_PROMPT - 1, T_PROMPT - 2), (T_PROMPT, T_PROMPT + 1), (T - 1, T - 2)):
                    last = nc.vector.tensor_copy(xx[:, :, at:at + 1], h[:, :, neighbour:neighbour + 1])
                    last.then_inc(step, 1)
                dve.wait_ge(step, 5)
                for k in range(KT):
                    nc.vector.scalar_tensor_tensor(xx[:, k], xx[:, k], 0.5, h[:, k], ALU.mult, ALU.subtract)


def mixed_product(nc, name, h, xx, mu, sources, func, out, out_tile, xh, xl):
    n, load_tile, zero_first = sources
    with Phase(nc, name) as ph:
        raw = ph.sb("raw", [P, 2, KT, P])
        wh = ph.sb("wh", [P, 2, KT, P], F32R)
        wl = ph.sb("wl", [P, 2, KT, P], F32R)
        mixed = ph.sb("mixed", [P, 2, T])
        mus = ph.sb("mus", [P, KT])
        ot = ph.sb("ot", [P, 2, T])
        ps = ph.ps("ps", [P, 2, 3, 512])
        w_in, stored, mu_in = ph.sems("w_in", 2), ph.sems("stored", 2), ph.sem("mu_in")
        hi_done, lo_done, prod_done, out_done = (ph.sem(x) for x in ("hi_done", "lo_done", "prod_done", "out_done"))
        mix_done, mix_hi, mix_lo, cleared = (ph.sem(x) for x in ("mix_done", "mix_hi", "mix_lo", "cleared"))
        rounds = n // 2 if n > 1 else 0
        with nc.Block() as block:
            @block.sync
            def _(sp):
                with nc.allow_non_contiguous_dma("mix weights by channel"):
                    sp.dma_start(mus[:], mu.rearrange("(k p) -> p k", p=P)).then_inc(mu_in, 16)
                sp.sem_inc(lo_done, CREDIT)
                if zero_first:
                    sp.wait_ge(cleared, 1)
                if rounds:
                    with sp.Fori(0, rounds) as j:
                        for s in range(2):
                            sp.wait_ge(lo_done, j * 2 + (s + 1))
                            load_tile(sp, j, s, raw).then_inc(w_in[s], 16)
                else:
                    load_tile(sp, 0, 0, raw).then_inc(w_in[0], 16)

            @block.vector
            def _(dve):
                dve.wait_ge(mu_in, 16)
                for k in range(KT):
                    if k >= 2:
                        dve.wait_ge(mix_lo, k - 1)
                    nc.vector.scalar_tensor_tensor(mixed[:, k % 2], xx[:, k], mus[:, k:k + 1], h[:, k],
                                                   ALU.mult, ALU.add).then_inc(mix_done, 1)
                    dve.wait_ge(mix_hi, k + 1)
                    nc.vector.tensor_tensor(xl[:, k], mixed[:, k % 2], xh[:, k].bitcast(F32), ALU.subtract).then_inc(mix_lo, 1)

            @block.gpsimd
            def _(pool):
                if zero_first:
                    nc.gpsimd.memset(raw[:], 0.0).then_inc(cleared, 1)
                if rounds:
                    with pool.Fori(0, rounds) as j:
                        for s in range(2):
                            pool.wait_ge(hi_done, j * 2 + (s + 1))
                            nc.gpsimd.tensor_tensor(wl[:, s], raw[:, s], wh[:, s].bitcast(F32), ALU.subtract).then_inc(lo_done, 1)
                else:
                    pool.wait_ge(hi_done, 1)
                    nc.gpsimd.tensor_tensor(wl[:, 0], raw[:, 0], wh[:, 0].bitcast(F32), ALU.subtract).then_inc(lo_done, 1)

            @block.scalar
            def _(act):
                for s in range(2):
                    act.sem_inc(stored[s], 16)
                act.sem_inc(prod_done, CREDIT)

                def cut(j, s, i):
                    act.wait_ge(w_in[s], j * 16 + 16)
                    act.wait_ge(prod_done, i + 1)
                    nc.scalar.activation(wh[:, s], raw[:, s], ACT.Copy).then_inc(hi_done, 1)

                cut(0, 0, 0)
                for k in range(KT):
                    act.wait_ge(mix_done, k + 1)
                    nc.scalar.activation(xh[:, k], mixed[:, k % 2], ACT.Copy).then_inc(mix_hi, 1)

                def leave(j, s, i):
                    act.wait_ge(prod_done, i + (1 + CREDIT))
                    act.wait_ge(stored[s], j * 16 + 16)
                    nc.scalar.activation(ot[:, s, 0:1024], ps[:, s, 0:2].rearrange("p g n -> p (g n)"), func)
                    nc.scalar.activation(ot[:, s, 1024:1280], ps[:, s, 2, 0:256], func).then_inc(out_done, 1)
                    act.wait_ge(out_done, i + (1 + CREDIT))
                    act.dma_start(out[:, bass.ds(i + out_tile, 1), :].rearrange("p a t -> p (a t)"), ot[:, s]).then_inc(stored[s], 16)

                if rounds > 1:
                    with act.Fori(0, rounds - 1) as j:
                        cut(j, 1, j * 2 + 1)
                        leave(j, 0, j * 2)
                        cut(j + 1, 0, j * 2 + 2)
                        leave(j, 1, j * 2 + 1)
                if rounds:
                    cut(rounds - 1, 1, n - 1)
                    leave(rounds - 1, 0, n - 2)
                    leave(rounds - 1, 1, n - 1)
                else:
                    leave(0, 0, 0)
                for s in range(2):
                    act.wait_ge(stored[s], 16 * (1 + (rounds if rounds else 1 - s)))

            @block.tensor
            def _(pe):
                pe.sem_inc(out_done, CREDIT)
                pe.wait_ge(mix_lo, KT)

                def product(i, s):
                    pe.wait_ge(lo_done, i + (1 + CREDIT))
                    pe.wait_ge(out_done, i + 1)
                    product_tile(nc, ps[:, s], wh[:, s], wl[:, s], xh, xl, KT).then_inc(prod_done, 1)

                if rounds:
                    with pe.Fori(0, rounds) as j:
                        for s in range(2):
                            product(j * 2 + s, s)
                else:
                    product(0, 0)


def rwkv_inputs(nc, xres, gain, mu, w_r, w_k, w_v, w1, a1, g1, rkv, lora, consts):
    def square(w):
        wv = w.rearrange("(k p) n -> p k n", p=P)
        return 8, lambda eng, j, s, raw: eng.dma_start(raw[:, s], wv[:, :, bass.ds(j * 2 * P + s * P, P)]), False

    def pair_source(w):
        wv = w.rearrange("(k p) n -> p k n", p=P)
        return 1, lambda eng, j, s, raw: eng.dma_start(raw[:, s], wv), False

    with Phase(nc, "ri") as ph:
        h = ph.sb("h", [P, KT, T])
        rms_norm(nc, "rn", xres, gain, consts, h, None)
        xx = ph.sb("xx", [P, KT, T])
        xh = ph.sb("xh", [P, KT, T], F32R)
        xl = ph.sb("xl", [P, KT, T], F32R)
        mix_differences(nc, h, xx)
        mixed_product(nc, "pr", h, xx, mu[0], square(w_r), ACT.Copy, rkv, 0, xh, xl)
        mixed_product(nc, "pk", h, xx, mu[2], square(w_k), ACT.Copy, rkv, 8, xh, xl)
        mixed_product(nc, "pv", h, xx, mu[3], square(w_v), ACT.Copy, rkv, 16, xh, xl)

        mixed_product(nc, "pw", h, xx, mu[1], pair_source(w1), ACT.Tanh, lora, 0, xh, xl)
        mixed_product(nc, "pa", h, xx, mu[4], pair_source(a1), ACT.Copy, lora, 1, xh, xl)
        gv = g1.rearrange("(k p) n -> p k n", p=P)
        rest = g1.shape[1] - P
        mixed_product(nc, "pg", h, xx, mu[5],
                      (2, lambda eng, j, s, raw: eng.dma_start(raw[:, s, :, 0:(P, rest)[s]], gv[:, :, s * P:s * P + (P, rest)[s]]), True),
                      ACT.Sigmoid, lora, 2, xh, xl)



C = 64
NC = T // C
NCP = T_PROMPT // C
LEVELS = 6
DECAY = float(2.718281828459045 ** -0.5)
Z = 2


class Count:

    def __init__(self, sem, credit=1, per=1):
        self.sem, self.credit, self.per = sem, credit, per

    def after(self, n):
        return n + self.credit


def rwkv_scan(nc, rkv, lora, w0, w2, a0, a2, k_k, k_a, r_k, ysc, bsc, consts):
    E_TILES = 6
    ND = 32
    with Phase(nc, "sc") as ph:
        ident = ph.sb("ident", [P, P])
        block64 = ph.sb("block64", [P, P])
        eye2 = ph.sb("eye2", [P, Z, C])
        m_strict = ph.sb("m_strict", [P, Z, C])
        m_incl = ph.sb("m_incl", [P, Z, C])
        m_level = ph.sb("m_level", [P, LEVELS, Z, C])
        keep = ph.sb("keep", [P, Z, NC])
        prm = ph.sb("prm", [P, 8, PAIRS])
        restart = ph.sb("restart", [P, T])
        tl = ph.sb("tl", [P, 2, T])
        w2t = ph.sb("w2t", [P, P])
        a2t = ph.sb("a2t", [P, P])
        rkvt = ph.sb("rkvt", [P, 3, T])
        sg = ph.sb("sg", [P, Z, T])
        cum = ph.sb("cum", [P, Z, T])
        xb = ph.sb("xb", [P, T])
        aa = ph.sb("aa", [P, Z, T])
        kd = ph.sb("kd", [P, Z, T])
        kkn = ph.sb("kkn", [P, T])
        tmp = ph.sb("tmp", [P, T])
        ex = ph.sb("ex", [P, 2, T])
        kb = ph.sb("kb", [P, Z, NC, 2, C])
        ar = ph.sb("ar", [P, Z, NC, 2, C])
        pc = ph.sb("pc", [P, Z, NC])
        yt = ph.sb("yt", [P, T])
        bo = ph.sb("bo", [P, T])
        kbs = ph.sb("kbs", [P, 2, Z, 3, C])
        ws = ph.sb("ws", [P, 2, Z, 4, C])
        vv = ph.sb("vv", [P, 2, Z, 2, C])
        pcs = ph.sb("pcs", [P, 2, Z])
        tt = ph.sb("tt", [P, 2, 2, Z, 2, C])
        nr = ph.sb("nr", [P, 2, 2, Z, C])
        bm = ph.sb("bm", [P, Z, C])
        bl = ph.sb("bl", [P, 2, LEVELS, Z, C])
        trt = ph.sb("trt", [P, 2, 2, Z, C])
        rf = ph.sb("rf", [P, 2, Z, C])
        pt = ph.sb("pt", [P, Z, C])
        xs = ph.sb("xs", [P, Z, C])
        st = ph.sb("st", [P, 2, Z, C])
        snew = ph.sb("snew", [P, Z, C])
        banks = [ph.ps(f"bank{i}", [P, 3, 512]) for i in range(2)]
        bank6, bank7 = ph.ps("bank6", [P, 3, Z, C]), ph.ps("bank7", [P, Z, C])
        turn = (banks[0][:, 0, 0:256], banks[0][:, 1, 0:256])
        gram = (banks[0][:, 2, 0:256].rearrange("p (z n) -> p z n", z=Z),
                banks[1][:, 0, 0:256].rearrange("p (z n) -> p z n", z=Z))
        pbank = banks[1][:, 1, 0:Z * C].rearrange("p (z n) -> p z n", z=Z)
        trbank = banks[1][:, 2, 0:2 * Z * C].rearrange("p (a z n) -> p a z n", a=2, z=Z)
        halves = (slice(0, HD), slice(HD, P))

        small_in, zeroed = ph.sem("small_in"), ph.sem("zeroed")
        pair_in, prep_pe, prep_act, prep_dve, stored = (ph.sem(x) for x in ("pair_in", "prep_pe", "prep_act", "prep_dve", "stored"))
        names = ("staged tr_done tt_out gram_done gram_out lv_done t2_done t_init p_done p_out tr2_done tr2_out "
                 "u_init x_done x_out u_done u_out s_done y_done s_out y_out s_tmp").split()
        S = {x: ph.sem(x) for x in names}
        held = ph.sem("held")
        CR = 2

        def chunks(t):
            return t.rearrange("p (c n) -> p c n", n=C)

        def chunk_of(z, c):
            return c if z == 0 else (NC - 1) - c

        def steps(eng, p, body):
            with eng.Fori(0, NC // 2 - 1) as j:
                for s in range(2):
                    body(p * NC + (j * 2 + s), j * 2 + s, s, True, True)
            body(p * NC + (NC - 2), NC - 2, 0, True, False)
            body(p * NC + (NC - 1), NC - 1, 1, False, False)

        with nc.Block() as block:
            @block.sync
            def _(sp):
                loads = [(ident, consts["ident"]), (block64, consts["block64"]), (eye2, consts["eye2"]), (m_strict, consts["m_strict"]),
                         (m_incl, consts["m_incl"]), (m_level, consts["m_level"]), (keep, consts["keep"]), (tl, lora[:, 0:2])]
                for dst, src in loads:
                    sp.dma_start(dst[:], src).then_inc(small_in, 16)
                with nc.allow_non_contiguous_dma("parameters by channel"):
                    for i, q in enumerate((w0[0], w0[1], a0[0], a0[1], k_k, k_a, r_k)):
                        sp.dma_start(prm[:, i, :], q.rearrange("(k p) -> p k", p=P)).then_inc(small_in, 16)
                with sp.Fori(0, PAIRS) as p:
                    sp.wait_ge(S["y_out"], p * NC + CR)
                    for i in range(3):
                        sp.dma_start(rkvt[:, i], rkv[:, bass.ds(p + i * KT, 1), :].rearrange("p a t -> p (a t)")).then_inc(pair_in, 16)
                    sp.dma_start(w2t[:], w2[:, bass.ds(p * P, P)]).then_inc(pair_in, 16)
                    sp.dma_start(a2t[:], a2[:, bass.ds(p * P, P)]).then_inc(pair_in, 16)
                    sp.wait_ge(prep_dve, p * ND + ND)
                    sp.dma_start(bsc[:, bass.ds(p, 1), :].rearrange("p a t -> p (a t)"), bo[:]).then_inc(stored, 16)
                    sp.wait_ge(S["y_out"], p * NC + (NC + CR))
                    sp.dma_start(ysc[:, bass.ds(p, 1), :].rearrange("p a t -> p (a t)"), yt[:]).then_inc(stored, 16)
                    sp.wait_ge(stored, p * 32 + 32)
                    sp.sem_inc(held, 1)

            @block.gpsimd
            def _(pool):
                for x in ("y_done",):
                    pool.sem_inc(S[x], CR)
                pool.wait_ge(small_in, 16 * 15)
                pool.wait_ge(zeroed, 1)

                def stage(g, c, s):
                    pool.wait_ge(S["y_done"], g + (CR - 1))
                    pool.wait_ge(S["s_out"], g + (CR - 1))
                    pool.sem_inc(held, 1)
                    for z in range(Z):
                        cz = chunk_of(z, c)
                        src = kb[:, z, bass.ds(cz, 1)].rearrange("p a b n -> p (a b) n")
                        nc.gpsimd.tensor_copy(kbs[:, s, z, 0:2, :], src)
                        nc.gpsimd.tensor_copy(kbs[:, s, z, 2:3, :], kb[:, z, bass.ds(cz, 1), 0, :])
                        src = ar[:, z, bass.ds(cz, 1)].rearrange("p a b n -> p (a b) n")
                        for i in range(2):
                            nc.gpsimd.tensor_copy(ws[:, s, z, 2 * i:2 * i + 2, :], src)
                        nc.gpsimd.tensor_copy(pcs[:, s, z:z + 1], pc[:, z, bass.ds(cz, 1)])
                        last = nc.gpsimd.tensor_copy(vv[:, s, z], rkvt[:, 2:3, bass.ds(cz * C, C)].to_broadcast([P, 2, C]))
                    last.then_inc(S["staged"], 1)

                def levels(g, s):
                    pool.wait_ge(S["gram_out"], g + (1 + CR))
                    b = bm[:].rearrange("p (a z) n -> p a z n", a=1).to_broadcast([P, LEVELS, Z, C])
                    nc.gpsimd.tensor_tensor(bl[:, s], b, m_level[:], ALU.mult).then_inc(zeroed, 1)
                    pool.wait_ge(zeroed, g + 2)
                    nc.gpsimd.tensor_tensor(trt[:, s, 1], bl[:, s, 0], eye2[:], ALU.add).then_inc(S["lv_done"], 1)

                with pool.Fori(0, PAIRS) as p:
                    pool.wait_ge(prep_dve, p * ND + ND)
                    stage(p * NC, 0, 0)
                    levels(p * NC, 0)
                    stage(p * NC + 1, 1, 1)

                    def body(g, c, s, more, more2):
                        if more:
                            levels(g + 1, 1 - s)
                        if more2:
                            stage(g + 2, c + 2, s)
                    steps(pool, p, body)

            @block.tensor
            def _(pe):
                for x in ("tt_out", "gram_out", "t_init", "p_out", "tr2_out", "x_out", "y_out"):
                    pe.sem_inc(S[x], CR)
                pe.wait_ge(small_in, 16 * 15)

                def turn_and_gram(g, s):
                    pe.wait_ge(S["staged"], g + 1)
                    pe.wait_ge(S["tt_out"], g + CR)
                    pe.sem_inc(held, 1)
                    for h in range(2):
                        rows = halves[h]
                        for z in range(Z):
                            nc.tensor.transpose(turn[h][:, z * 128:z * 128 + 64], kbs[rows, s, z, h:h + 2, :].rearrange("p a n -> p (a n)"),
                                                ident[rows, rows])
                            last = nc.tensor.transpose(turn[h][:, z * 128 + 64:z * 128 + 128], vv[rows, s, z].rearrange("p a n -> p (a n)"),
                                                       ident[rows, rows])
                    last.then_inc(S["tr_done"], 1)
                    pe.wait_ge(S["gram_out"], g + CR)
                    for h in range(2):
                        rows = halves[h]
                        for z in range(Z):
                            last = nc.tensor.matmul(gram[h][:, z, :], kbs[rows, s, z, h:h + 2, :].rearrange("p a n -> p (a n)"),
                                                    ws[rows, s, z, 2 * h:2 * h + 2, :].rearrange("p a n -> p (a n)"), start=True, stop=True)
                    last.then_inc(S["gram_done"], 1)

                def t2(g, s):
                    pe.wait_ge(S["lv_done"], g + 1)
                    pe.wait_ge(S["tr2_out"], g * 5 + CR)
                    pe.sem_inc(held, 1)
                    for z in range(Z):
                        for rows in halves:
                            last = nc.tensor.matmul(trbank[rows, 0, z], trt[rows, s, 1, z], eye2[rows, 0], start=True, stop=True)
                    last.then_inc(S["t2_done"], 1)

                def level_p(g, s, k):
                    if k == 0:
                        pe.wait_ge(S["t_init"], g + (1 + CR))
                    else:
                        pe.wait_ge(S["tr2_out"], g * 5 + (k + CR))
                    pe.wait_ge(S["p_out"], g * 5 + (k + CR))
                    pe.sem_inc(held, 1)
                    for z in range(Z):
                        for rows in halves:
                            last = nc.tensor.matmul(pbank[rows, z], bl[rows, s, k + 1, z], trt[rows, s, 0, z], start=True, stop=True)
                    last.then_inc(S["p_done"], 1)

                def level_tr(g, s, k):
                    pe.wait_ge(S["p_out"], g * 5 + (k + 1 + CR))
                    pe.sem_inc(held, 1)
                    for z in range(Z):
                        for rows in halves:
                            if k < 4:
                                nc.tensor.matmul(trbank[rows, 0, z], trt[rows, s, 1, z], pt[rows, z], start=True, stop=True)
                            last = nc.tensor.matmul(trbank[rows, 1, z], pt[rows, z], trt[rows, s, 1, z], start=True, stop=True)
                    last.then_inc(S["tr2_done"], 1)

                def x_product(g, s):
                    pe.wait_ge(S["u_init"], g + 1)
                    pe.wait_ge(S["gram_out"], g + (1 + CR))
                    for z in range(Z):
                        for h in range(2):
                            last = nc.tensor.matmul(bank6[halves[h], 0, z], ws[:, s, z, 2 * h], tt[:, s, h, z, 1], start=True, stop=True)
                    last.then_inc(S["x_done"], 1)

                def u_product(g, s):
                    pe.wait_ge(S["x_out"], g + (1 + CR))
                    pe.wait_ge(S["tr2_out"], g * 5 + (5 + CR))
                    pe.sem_inc(held, 1)
                    for z in range(Z):
                        for h in range(2):
                            last = nc.tensor.matmul(bank6[halves[h], 1, z], rf[halves[h], s, z], xs[halves[h], z], start=True, stop=True)
                    last.then_inc(S["u_done"], 1)

                def s_and_y(g, s):
                    pe.wait_ge(S["u_out"], g + 1)
                    for z in range(Z):
                        for h in range(2):
                            last = nc.tensor.matmul(bank6[halves[h], 2, z], tt[:, s, h, z, 0], tt[:, s, h, z, 1], start=True, stop=True)
                    last.then_inc(S["s_done"], 1)
                    pe.wait_ge(S["y_out"], g + CR)
                    pe.sem_inc(held, 1)
                    for z in range(Z):
                        for h in range(2):
                            rows = halves[h]
                            nc.tensor.matmul(bank7[rows, z], st[rows, s, z], ws[rows, s, z, 2 * h + 1], start=True, stop=False)
                            last = nc.tensor.matmul(bank7[rows, z], tt[:, s, h, z, 1], nr[:, s, h, z], start=False, stop=True)
                    last.then_inc(S["y_done"], 1)

                with pe.Fori(0, PAIRS) as p:
                    pe.wait_ge(pair_in, p * 80 + 80)
                    pe.wait_ge(S["y_out"], p * NC + CR)
                    for i in range(6):
                        bank = banks[i % 2]
                        if i in (2, 3):
                            pe.wait_ge(prep_act, p * 13 + (i - 1))
                        if i == 4:
                            pe.wait_ge(prep_act, p * 13 + 5)
                        if i == 5:
                            pe.wait_ge(prep_dve, p * ND + 18)
                        for gi, (t0, n) in enumerate(TOK_GROUPS):
                            if i < 4:
                                z = i % 2
                                w = (w2t, a2t)[i // 2]
                                last = nc.tensor.matmul(bank[:, gi, 0:n], w[halves[z]], tl[halves[z], i // 2, t0:t0 + n], start=True, stop=True)
                            else:
                                src = (tmp, xb)[i - 4]
                                last = nc.tensor.matmul(bank[:, gi, 0:n], block64[:], src[:, t0:t0 + n], start=True, stop=True)
                        last.then_inc(prep_pe, 1)
                    pe.wait_ge(prep_dve, p * ND + ND)

                    def prepare(g, s):
                        t2(g, s)
                        for k in range(5):
                            level_p(g, s, k)
                            level_tr(g, s, k)

                    turn_and_gram(p * NC, 0)
                    prepare(p * NC, 0)

                    def body(g, c, s, more, more2):
                        x_product(g, s)
                        if more:
                            turn_and_gram(g + 1, 1 - s)
                        u_product(g, s)
                        if more:
                            t2(g + 1, 1 - s)
                            level_p(g + 1, 1 - s, 0)
                        s_and_y(g, s)
                        if more:
                            level_tr(g + 1, 1 - s, 0)
                            for k in range(1, 5):
                                level_p(g + 1, 1 - s, k)
                                level_tr(g + 1, 1 - s, k)
                    steps(pe, p, body)

            @block.scalar
            def _(act):
                act.wait_ge(small_in, 16 * 15)
                act.sem_inc(S["s_out"], CR)

                def tt_copy(g, s):
                    act.wait_ge(S["tr_done"], g + 1)
                    for h in range(2):
                        last = nc.scalar.activation(tt[:, s, h].rearrange("p z a n -> p (z a n)"), turn[h], ACT.Copy)
                    last.then_inc(S["tt_out"], 1)

                def t_first(g, s):
                    act.wait_ge(S["t2_done"], g + 1)
                    nc.scalar.activation(trt[:, s, 0], trbank[:, 0], ACT.Copy).then_inc(S["t_init"], 1)

                def p_copy(g, k):
                    act.wait_ge(S["p_done"], g * 5 + (k + 1))
                    nc.scalar.activation(pt[:], pbank, ACT.Copy).then_inc(S["p_out"], 1)

                def state_in(g, s):
                    act.wait_ge(S["s_out"], g + CR)
                    for h in range(2):
                        last = nc.scalar.activation(tt[halves[h], s, h, :, 1, :], st[halves[h], s], ACT.Copy)
                    last.then_inc(S["u_init"], 1)

                def x_copy(g):
                    act.wait_ge(S["x_done"], g + 1)
                    nc.scalar.activation(xs[:], bank6[:, 0], ACT.Copy).then_inc(S["x_out"], 1)

                def u_copy(g, s):
                    act.wait_ge(S["u_done"], g + 1)
                    for h in range(2):
                        last = nc.scalar.activation(tt[halves[h], s, h, :, 1, :], bank6[halves[h], 1], ACT.Copy)
                    last.then_inc(S["u_out"], 1)

                with act.Fori(0, PAIRS) as p:
                    def lora_out(i):
                        dst = (sg, aa)[i // 2][:, i % 2]
                        bias = prm[:, i, bass.ds(p, 1)]
                        bank = banks[i % 2]
                        act.wait_ge(prep_pe, p * 6 + (i + 1))
                        nc.scalar.activation(dst[:, 0:1024], bank[:, 0:2].rearrange("p g n -> p (g n)"), ACT.Sigmoid, bias=bias)
                        nc.scalar.activation(dst[:, 1024:1280], bank[:, 2, 0:256], ACT.Sigmoid, bias=bias).then_inc(prep_act, 1)
                    for i in range(4):
                        lora_out(i)
                    act.wait_ge(prep_dve, p * ND + 1)
                    nc.scalar.activation(tmp[:], kkn[:], ACT.Square).then_inc(prep_act, 1)
                    act.wait_ge(prep_pe, p * 6 + 5)
                    nc.scalar.activation(tmp[:, 0:1024], banks[0][:, 0:2].rearrange("p g n -> p (g n)"), ACT.Sqrt)
                    nc.scalar.activation(tmp[:, 1024:1280], banks[0][:, 2, 0:256], ACT.Sqrt).then_inc(prep_act, 1)
                    act.wait_ge(prep_dve, p * ND + 6)
                    sources = [(sg[:, 0], -DECAY), (cum[:, 0], -DECAY), (cum[:, 0], DECAY),
                               (cum[:, 1], -DECAY), (sg[:, 1], -DECAY), (sg[:, 1], DECAY)]
                    for i, (src, scale) in enumerate(sources):
                        if i >= 2:
                            act.wait_ge(prep_dve, p * ND + E_FREE[i - 2])
                        nc.scalar.activation(ex[:, i % 2], src, ACT.Exp, scale=scale).then_inc(prep_act, 1)
                    act.wait_ge(prep_dve, p * ND + ND)
                    nc.scalar.activation(pcs[0:1, 0, 0:1], pcs[0:1, 0, 0:1], ACT.Copy).then_inc(prep_act, 1) if False else act.sem_inc(prep_act, 1)

                    tt_copy(p * NC, 0)
                    t_first(p * NC, 0)
                    for k in range(5):
                        p_copy(p * NC, k)

                    def body(g, c, s, more, more2):
                        state_in(g, s)
                        x_copy(g)
                        if more:
                            tt_copy(g + 1, 1 - s)
                        u_copy(g, s)
                        if more:
                            t_first(g + 1, 1 - s)
                            for k in range(5):
                                p_copy(g + 1, k)
                    steps(act, p, body)

            @block.vector
            def _(dve):
                nc.vector.memset(st[:], 0.0)
                nc.vector.memset(restart[:], 1.0).then_inc(S["s_tmp"], 1)
                dve.wait_ge(S["s_tmp"], 1)
                dve.wait_ge(small_in, 16 * 15)
                nc.vector.tensor_scalar(prm[:, 7], prm[:, 5], -1.0, 1.0, ALU.mult, ALU.add)
                nc.vector.memset(chunks(restart[:])[:, :, 0:1], 0.0).then_inc(zeroed, 1)
                dve.wait_ge(zeroed, 1)

                def gram_out(g, s):
                    dve.wait_ge(S["gram_done"], g + 1)
                    dve.wait_ge(S["lv_done"], g) if not isinstance(g, int) else None
                    for h in range(2):
                        nc.vector.tensor_tensor(bm[halves[h]], gram[h][halves[h], :, 0:C], m_strict[halves[h]], ALU.mult)
                    for h in range(2):
                        nc.vector.tensor_tensor(nr[:, s, h], gram[h][:, :, C:2 * C], m_incl[:], ALU.mult)
                        o = halves[1 - h]
                        last = nc.vector.tensor_tensor(ws[o, s, :, 2 * h, :], gram[h][o, :, 0:C], m_strict[o], ALU.mult)
                    last.then_inc(S["gram_out"], 1)

                def tr_out(g, s, k):
                    dve.wait_ge(S["tr2_done"], g * 5 + (k + 1))
                    if k < 4:
                        nc.vector.tensor_tensor(trt[:, s].rearrange("p a z n -> p (a z n)"), trbank.rearrange("p a z n -> p (a z n)"),
                                                trt[:, s].rearrange("p a z n -> p (a z n)"), ALU.add).then_inc(S["tr2_out"], 1)
                    else:
                        nc.vector.tensor_tensor(rf[:, s], trbank[:, 1], trt[:, s, 1], ALU.add).then_inc(S["tr2_out"], 1)

                def state_out(g, c, s):
                    dve.wait_ge(S["s_done"], g + 1)
                    nc.vector.tensor_tensor(snew[:], bank6[:, 2], st[:, s], ALU.add).then_inc(S["s_tmp"], 1)
                    dve.wait_ge(S["s_tmp"], g + 2)
                    nc.vector.tensor_tensor(st[:, 1 - s], snew[:], pcs[:, s].rearrange("p (z a) -> p z a", a=1).to_broadcast([P, Z, C]),
                                            ALU.mult).then_inc(S["s_out"], 1)
                    dve.wait_ge(S["y_done"], g + (1 + CR))
                    for z in range(Z):
                        y = yt[:, bass.ds(chunk_of(z, c) * C, C)]
                        last = nc.vector.tensor_tensor(y, bank7[:, z], y, ALU.add)
                    last.then_inc(S["y_out"], 1)

                with dve.Fori(0, PAIRS) as p:
                    n = [0]

                    def d(ins):
                        n[0] += 1
                        ins.then_inc(prep_dve, 1)
                        return n[0]

                    def own(at):
                        dve.wait_ge(prep_dve, p * ND + at)

                    pp = lambda i: prm[:, i, bass.ds(p, 1)]
                    r_, k_, v_ = rkvt[:, 0], rkvt[:, 1], rkvt[:, 2]
                    dve.wait_ge(pair_in, p * 80 + 80)
                    a_kk = d(nc.vector.tensor_scalar(kkn[:], k_, pp(4), None, ALU.mult))
                    for z in range(Z):
                        dve.wait_ge(prep_act, p * 13 + (z + 1))
                        d(nc.vector.tensor_tensor_scan(cum[:, z], restart[:], sg[:, z], 0.0, ALU.mult, ALU.add))
                    own(3)
                    d(nc.vector.tensor_tensor(sg[:, 0], cum[:, 0], sg[:, 0], ALU.subtract))
                    tot = chunks(cum[:, 1])[:, :, C - 1:C].to_broadcast([P, NC, C])
                    d(nc.vector.tensor_tensor(chunks(xb[:]), tot, chunks(cum[:, 1]), ALU.subtract))
                    own(5)
                    nc.vector.tensor_copy(cum[:, 1], xb[:])
                    d(nc.vector.tensor_tensor(sg[:, 1], xb[:], sg[:, 1], ALU.add))
                    dve.wait_ge(prep_act, p * 13 + 6)
                    x = d(nc.vector.tensor_scalar(tmp[:], tmp[:], 1e-12, None, ALU.max))
                    own(x)
                    x = d(nc.vector.reciprocal(tmp[:], tmp[:]))
                    own(x)
                    x = d(nc.vector.tensor_tensor(kkn[:], kkn[:], tmp[:], ALU.mult))
                    for z in range(Z):
                        d(nc.vector.tensor_scalar(kd[:, z], aa[:, z], pp(5), pp(7), ALU.mult, ALU.add))
                    own(11)
                    for z in range(Z):
                        d(nc.vector.tensor_tensor(aa[:, z], aa[:, z], kkn[:], ALU.mult))
                        d(nc.vector.tensor_tensor(kd[:, z], kd[:, z], k_, ALU.mult))
                    own(15)
                    d(nc.vector.tensor_tensor(xb[:], kd[:, 0], kd[:, 1], ALU.add))
                    own(16)
                    d(nc.vector.scalar_tensor_tensor(xb[:], xb[:], pp(6), r_, ALU.mult, ALU.mult))
                    d(nc.vector.memset(yt[:], 0.0))
                    for z in range(Z):
                        for i in range(3):
                            e = ex[:, (3 * z + i) % 2]
                            dve.wait_ge(prep_act, p * 13 + (7 + 3 * z + i))
                            if i == 0:
                                d(nc.vector.scalar_tensor_tensor(ar[:, z, :, 0, :], chunks(e), -1.0, chunks(kkn[:]), ALU.mult, ALU.mult))
                            elif i == 1:
                                d(nc.vector.tensor_tensor(ar[:, z, :, 1, :], chunks(r_), chunks(e), ALU.mult))
                                at = (C - 1, 0)[z]
                                d(nc.vector.tensor_tensor(pc[:, z], chunks(e)[:, :, at], keep[:, z], ALU.mult))
                            else:
                                d(nc.vector.tensor_tensor(kb[:, z, :, 0, :], chunks(aa[:, z]), chunks(e), ALU.mult))
                                d(nc.vector.tensor_tensor(kb[:, z, :, 1, :], chunks(kd[:, z]), chunks(e), ALU.mult))
                    dve.wait_ge(prep_pe, p * 6 + 6)
                    d(nc.vector.tensor_tensor(bo[:, 0:1024], banks[1][:, 0:2].rearrange("p g n -> p (g n)"), v_[:, 0:1024], ALU.mult))
                    d(nc.vector.tensor_tensor(bo[:, 1024:1280], banks[1][:, 2, 0:256], v_[:, 1024:1280], ALU.mult))
                    while n[0] < ND - 1:
                        n[0] += 1
                        dve.sem_inc(prep_dve, 1)
                    own(30)
                    dve.sem_inc(held, 1)
                    assert n[0] == ND - 1
                    dve.drain().then_inc(prep_dve, 1)

                    gram_out(p * NC, 0)
                    for k in range(5):
                        tr_out(p * NC, 0, k)

                    def body(g, c, s, more, more2):
                        if more:
                            gram_out(g + 1, 1 - s)
                        state_out(g, c, s)
                        if more:
                            for k in range(5):
                                tr_out(g + 1, 1 - s, k)
                    steps(dve, p, body)


E_FREE = (19, 21, 23, 24)


def rwkv_gate(nc, ysc, bsc, lora, g2, ln_w, ln_b, consts, oh, ol):
    rest = g2.shape[0] - P
    ND = 9
    with Phase(nc, "rg") as ph:
        block64 = ph.sb("block64", [P, P])
        gl = ph.sb("gl", [P, 2, T])
        g2a = ph.sb("g2a", [P, D])
        g2b = ph.sb("g2b", [rest, D])
        prm = ph.sb("prm", [P, 2, KT])
        yt = ph.sb("yt", [P, T])
        bt = ph.sb("bt", [P, T])
        sq = ph.sb("sq", [P, T])
        ps = ph.ps("ps", [P, 2, 3, 512])
        small_in, y_in, act_n, pe_n, dve_n = (ph.sem(x) for x in ("small_in", "y_in", "act_n", "pe_n", "dve_n"))
        with nc.Block() as block:
            @block.sync
            def _(sp):
                loads = [(block64[:], consts["block64"]), (gl[:], lora[:, 2:4]), (g2a[:], g2[0:P]), (g2b[:], g2[P:P + rest])]
                for dst, src in loads:
                    sp.dma_start(dst, src).then_inc(small_in, 16)
                with nc.allow_non_contiguous_dma("parameters by channel"):
                    for i, q in enumerate((ln_w, ln_b)):
                        sp.dma_start(prm[:, i, :], q.rearrange("(k p) -> p k", p=P)).then_inc(small_in, 16)
                for p in range(PAIRS):
                    if p:
                        sp.wait_ge(act_n, p * 3)
                        sp.wait_ge(dve_n, p * ND)
                    sp.dma_start(yt[:], ysc[:, p]).then_inc(y_in, 16)
                    sp.dma_start(bt[:], bsc[:, p]).then_inc(y_in, 16)

            @block.tensor
            def _(pe):
                pe.wait_ge(small_in, 96)
                for p in range(PAIRS):
                    pe.wait_ge(y_in, p * 32 + 32)
                    if p:
                        pe.wait_ge(dve_n, p * ND)
                    for g, (t0, n) in enumerate(TOK_GROUPS):
                        last = nc.tensor.matmul(ps[:, 0, g, 0:n], block64[:], yt[:, t0:t0 + n], start=True, stop=True)
                    last.then_inc(pe_n, 1)
                    for g, (t0, n) in enumerate(TOK_GROUPS):
                        nc.tensor.matmul(ps[:, 1, g, 0:n], g2a[:, p * P:(p + 1) * P], gl[:, 0, t0:t0 + n], start=True, stop=False)
                        last = nc.tensor.matmul(ps[:, 1, g, 0:n], g2b[:, p * P:(p + 1) * P], gl[0:rest, 1, t0:t0 + n], start=False, stop=True)
                    last.then_inc(pe_n, 1)
                    pe.wait_ge(act_n, p * 3 + 1)
                    for g, (t0, n) in enumerate(TOK_GROUPS):
                        last = nc.tensor.matmul(ps[:, 0, g, 0:n], block64[:], sq[:, t0:t0 + n], start=True, stop=True)
                    last.then_inc(pe_n, 1)

            @block.scalar
            def _(act):
                for p in range(PAIRS):
                    act.wait_ge(dve_n, p * ND + 1)
                    nc.scalar.activation(sq[:], yt[:], ACT.Square).then_inc(act_n, 1)
                    act.wait_ge(dve_n, p * ND + 2)
                    nc.scalar.activation(sq[:], sq[:], ACT.Sqrt).then_inc(act_n, 1)
                    act.wait_ge(dve_n, p * ND + 8)
                    nc.scalar.activation(oh[:, p], yt[:], ACT.Copy).then_inc(act_n, 1)

            @block.vector
            def _(dve):
                dve.wait_ge(small_in, 96)
                flat = lambda b, s: b[:, s, 0:2].rearrange("p g n -> p (g n)")
                for p in range(PAIRS):
                    n = [p * ND]

                    def d(ins):
                        n[0] += 1
                        ins.then_inc(dve_n, 1)
                        dve.wait_ge(dve_n, n[0])

                    dve.wait_ge(pe_n, p * 3 + 1)
                    nc.vector.scalar_tensor_tensor(yt[:, 0:1024], flat(ps, 0), -1.0 / HD, yt[:, 0:1024], ALU.mult, ALU.add)
                    d(nc.vector.scalar_tensor_tensor(yt[:, 1024:T], ps[:, 0, 2, 0:256], -1.0 / HD, yt[:, 1024:T], ALU.mult, ALU.add))
                    dve.wait_ge(pe_n, p * 3 + 3)
                    nc.vector.tensor_scalar(sq[:, 0:1024], flat(ps, 0), 1.0 / HD, GN_EPS, ALU.mult, ALU.add)
                    d(nc.vector.tensor_scalar(sq[:, 1024:T], ps[:, 0, 2, 0:256], 1.0 / HD, GN_EPS, ALU.mult, ALU.add))
                    dve.wait_ge(act_n, p * 3 + 2)
                    d(nc.vector.reciprocal(sq[:], sq[:]))
                    d(nc.vector.scalar_tensor_tensor(yt[:], yt[:], prm[:, 0, p:p + 1], sq[:], ALU.mult, ALU.mult))
                    d(nc.vector.scalar_tensor_tensor(yt[:], yt[:], prm[:, 1, p:p + 1], bt[:], ALU.add, ALU.add))
                    d(nc.vector.tensor_tensor(yt[:, 0:1024], flat(ps, 1), yt[:, 0:1024], ALU.mult))
                    d(nc.vector.tensor_tensor(yt[:, 1024:T], ps[:, 1, 2, 0:256], yt[:, 1024:T], ALU.mult))
                    n[0] += 1
                    dve.drain().then_inc(dve_n, 1)
                    dve.wait_ge(act_n, p * 3 + 3)
                    d(nc.vector.tensor_tensor(ol[:, p], yt[:], oh[:, p].bitcast(F32), ALU.subtract))


def rwkv_layer(nc, xres, gain, mu, w_r, w_k, w_v, w_o, w0, w1, w2, a0, a1, a2, g1, g2, k_k, k_a, r_k, ln_w, ln_b,
               rkv, lora, ysc, bsc, consts):
    rwkv_inputs(nc, xres, gain, mu, w_r, w_k, w_v, w1, a1, g1, rkv, lora, consts)
    rwkv_scan(nc, rkv, lora, w0, w2, a0, a2, k_k, k_a, r_k, ysc, bsc, consts)
    with Phase(nc, "ro") as ph:
        oh = ph.sb("oh", [P, KT, T], F32R)
        ol = ph.sb("ol", [P, KT, T], F32R)
        rwkv_gate(nc, ysc, bsc, lora, g2, ln_w, ln_b, consts, oh, ol)
        residual_product(nc, "rw", w_o, KT, oh, ol, xres)



def shape_constants():
    import numpy as np
    c = np.arange(GRID_W)
    first = np.clip(c - WIN_W // 2, 0, GRID_W - WIN_W)
    seen = (c[None] >= first[:, None]) & (c[None] < first[:, None] + WIN_W)
    seen = np.tile(seen, (2, 1))
    i = np.arange(C)
    s, t = i[:, None], i[None, :]
    strict = np.stack([s < t, s > t])
    incl = np.stack([s <= t, s >= t])
    level = []
    for lv in range(LEVELS):
        n = 2 ** lv
        same = (s // (2 * n)) == (t // (2 * n))
        level.append(np.stack([same & (t % (2 * n) >= n) & (s % (2 * n) < n), same & (s % (2 * n) >= n) & (t % (2 * n) < n)]))
    keep = np.ones((Z, NC))
    keep[0, NCP - 1] = keep[0, NC - 1] = 0.0
    keep[1, NCP] = keep[1, 0] = 0.0
    two = lambda m: np.concatenate([m, m], 0)
    out = {
        "ident": np.eye(P),
        "ones": np.ones((P, P)),
        "block64": np.kron(np.eye(2), np.ones((HD, HD))),
        "colmask": np.stack([seen, np.where(seen, 0.0, NEG)], 1),
        "eye2": two(np.stack([np.eye(C)] * Z, 1)),
        "m_strict": two(strict.transpose(1, 0, 2)),
        "m_incl": two(incl.transpose(1, 0, 2)),
        "m_level": two(np.stack(level).transpose(2, 0, 1, 3)),
        "keep": np.broadcast_to(keep, (P, Z, NC)),
    }
    return {k: np.ascontiguousarray(v, dtype=np.float32) for k, v in out.items()}



CONSTS = ("ident", "ones", "block64", "colmask", "eye2", "m_strict", "m_incl", "m_level", "keep")


def trunk(nc, a, y):
    def scratch(name, shape):
        return nc.dram_tensor(name, shape, F32, kind="Internal").ap()

    consts = {k: a["c_" + k] for k in CONSTS}
    xres = scratch("xres", (P, KT, T))
    padded = scratch("padded", (PAIRS, 2, RPB_H, PADW))
    shifted_bias = scratch("shifted_bias", (PAIRS, 2, RPB_H, GRID_W, GRID_W))
    rkv, lora = scratch("rkv", (P, 3 * KT, T)), scratch("lora", (P, 4, T))
    ysc, bsc = scratch("ysc", (P, KT, T)), scratch("bsc", (P, KT, T))

    def mlp(i):
        ffn(nc, f"f{i}", xres, a["norm_ffn"][i], a["ffn_w_gate"][i], a["ffn_w_up"][i], a["ffn_conv_w"][i],
            a["ffn_conv_b"][i], a["ffn_w_down"][i], consts)

    transpose_in(nc, a["x"], xres, consts)
    attention_layer(nc, xres, a["norm_mix"][0], a["na_w_qkv"][0], a["na_w_o"][0], a["na_q_gain"][0],
                    a["na_k_gain"][0], a["na_rpb"][0], padded, shifted_bias, consts)
    mlp(0)
    rwkv_layer(nc, xres, a["norm_mix"][1], a["rw_mu"][0], a["rw_w_r"][0], a["rw_w_k"][0], a["rw_w_v"][0], a["rw_w_o"][0],
               a["rw_w0"][0], a["w1_pair"], a["rw_w2"][0].rearrange("z l d -> (z l) d"),
               a["rw_a0"][0], a["a1_pair"], a["rw_a2"][0].rearrange("z l d -> (z l) d"),
               a["rw_g1"][0], a["rw_g2"][0], a["rw_k_k"][0], a["rw_k_a"][0], a["rw_r_k"][0].rearrange("h n -> (h n)"),
               a["rw_ln_w"][0], a["rw_ln_b"][0], rkv, lora, ysc, bsc, consts)
    mlp(1)
    transpose_out(nc, xres, y, consts)


_WEIGHTS = ("norm_mix", "norm_ffn", "na_w_qkv", "na_w_o", "na_q_gain", "na_k_gain", "na_rpb", "rw_mu", "rw_w_r", "rw_w_k",
            "rw_w_v", "rw_w_o", "rw_w0", "rw_w2", "rw_a0", "rw_a2", "rw_g1", "rw_g2", "rw_k_k", "rw_k_a", "rw_r_k",
            "rw_ln_w", "rw_ln_b", "ffn_w_gate", "ffn_w_up", "ffn_conv_w", "ffn_conv_b", "ffn_w_down")


def kernel(**inputs):
    import numpy as np
    import concourse.bacc as bacc
    from concourse.bass_utils import run_bass_kernel_spmd

    given = {k: np.ascontiguousarray(inputs[k]) for k in _WEIGHTS}
    given["x"] = np.concatenate([np.asarray(inputs["x_prompt"])[0], np.asarray(inputs["x_sample"])[0]], 0)
    for name, source in (("w1_pair", "rw_w1"), ("a1_pair", "rw_a1")):
        w = np.asarray(inputs[source])[0]
        given[name] = np.concatenate([w[0], w[1]], 1)
    for k, v in shape_constants().items():
        given["c_" + k] = v

    nc = bacc.Bacc("TRN2", target_bir_lowering=False, num_devices=1)
    arrays, aps = {}, {}
    for name, v in given.items():
        arrays[f"in_{name}"] = np.ascontiguousarray(v)
        aps[name] = nc.dram_tensor(f"in_{name}", v.shape, mybir.dt.from_np(v.dtype), kind="ExternalInput").ap()
    y = nc.dram_tensor("y", (T, D), F32, kind="ExternalOutput").ap()
    trunk(nc, aps, y)
    out = run_bass_kernel_spmd(nc, [arrays], core_ids=[0]).results[0]["y"]
    return out[None, :T_PROMPT], out[None, T_PROMPT:]
```
